# Optimizing a Trainium2 kernel written in Bass

```python
import jax, jax.numpy as jnp
from jax import lax
import numpy as np

D_MODEL = 2048
BATCH = 1
SEQ = 256
DEPTH = 2
DEC_BATCH = 8
DEC_SEQ = 16
PAST_LEN = 512

CHUNK = 64
N_MIXERS = 2
N_SB_LAYERS = (DEPTH + 1) // 2
N_POOL_LAYERS = DEPTH // 2
N_HEADS = 16
HEAD_DIM = D_MODEL // N_HEADS
Q_BLOCK = 128
POOL_WINDOWS = (2, 4, 8, 16)
N_POOL_GROUPS = len(POOL_WINDOWS)
POOL_GROUP = D_MODEL // N_POOL_GROUPS
POOL_STATE = max(POOL_WINDOWS) - 1
D_FF = -(-8 * D_MODEL // (3 * 256)) * 256
N_MOD = 6
EPS = 1e-6

kernel_name = 'stickbreak_pool_streaming_encoder_step'

def rms_norm(x, g):
    xf = x.astype(jnp.float32)
    y = xf * lax.rsqrt(jnp.mean(xf * xf, axis=-1, keepdims=True) + EPS)
    return (y * g.astype(jnp.float32)).astype(x.dtype)

def ada_modulation(c, w, b):
    mod = jax.nn.silu(c) @ w + b
    return [m[:, None, :] for m in jnp.split(mod, N_MOD, axis=-1)]

def qkv_project(h, w_qkv, g_q, g_k):
    b, t, _ = h.shape
    qkv = (h @ w_qkv).reshape(b, t, 3, N_HEADS, HEAD_DIM)
    q = rms_norm(qkv[:, :, 0], g_q)
    k = rms_norm(qkv[:, :, 1], g_k)
    return q, k, qkv[:, :, 2]

def stick_breaking(q, k, v, q_pos, k_pos):
    z = jnp.einsum('bqhd,bkhd->bhqk', q, k, preferred_element_type=jnp.float32) * (HEAD_DIM ** -0.5)
    causal = k_pos[None, :] < q_pos[:, None]
    ls_neg = jax.nn.log_sigmoid(-z)
    log_1m = jnp.where(causal, ls_neg, 0.0)
    later = lax.cumsum(log_1m, axis=3, reverse=True) - log_1m
    weights = jnp.where(causal, jnp.exp(z + ls_neg + later), 0.0)
    return jnp.einsum('bhqk,bkhd->bqhd', weights.astype(v.dtype), v)

def sb_prompt(q, k, v):
    t = q.shape[1]
    outs = []
    for start in range(0, t, Q_BLOCK):
        end = min(start + Q_BLOCK, t)
        outs.append(stick_breaking(q[:, start:end], k[:, :end], v[:, :end],
                                   jnp.arange(start, end), jnp.arange(end)))
    return jnp.concatenate(outs, axis=1)

def sb_sample(q, k, v, k_past, v_past):
    p, t = k_past.shape[1], q.shape[1]
    k_all = jnp.concatenate([k_past, k], axis=1)
    v_all = jnp.concatenate([v_past, v], axis=1)
    return stick_breaking(q, k_all, v_all, p + jnp.arange(t), jnp.arange(p + t))

def pool_mixer(u, history, n_hist, w_pool, pool_scale):
    t = u.shape[1]
    seq = jnp.concatenate([history, u], axis=1)
    csum = jnp.cumsum(seq.astype(jnp.float32), axis=1)
    csum = jnp.pad(csum, ((0, 0), (1, 0), (0, 0)))
    csum_end = csum[:, POOL_STATE + 1:POOL_STATE + 1 + t]
    pos = jnp.arange(t)
    outs = []
    for g, w in enumerate(POOL_WINDOWS):
        sl = slice(g * POOL_GROUP, (g + 1) * POOL_GROUP)
        csum_start = csum[:, POOL_STATE + 1 - w:POOL_STATE + 1 - w + t, sl]
        count = jnp.minimum(n_hist + pos + 1, w).astype(jnp.float32)[None, :, None]
        mean = (csum_end[..., sl] - csum_start) / count
        diff = (mean - u[..., sl].astype(jnp.float32)).astype(u.dtype)
        outs.append(diff @ w_pool[g])
    out = jnp.concatenate(outs, axis=-1) * pool_scale
    return out, seq[:, -POOL_STATE:]

def swiglu(h, w_gate, w_up, w_down):
    return (jax.nn.silu(h @ w_gate) * (h @ w_up)) @ w_down

def trunk(x, c, k_cache, v_cache, pool_cache, w_ada, b_ada, g_mix, g_ffn, w_qkv, g_q, g_k, w_o,
          w_pool, pool_scale, w_gate, w_up, w_down):
    b, t, _ = x.shape
    is_sample = k_cache is not None
    n_hist = k_cache.shape[2] if is_sample else 0
    new_k, new_v, new_pool = [], [], []
    for i in range(DEPTH):
        shift1, scale1, gate1, shift2, scale2, gate2 = ada_modulation(c, w_ada[i], b_ada[i])
        h = rms_norm(x, g_mix[i]) * (1.0 + scale1) + shift1
        j = i // N_MIXERS
        if i % N_MIXERS == 0:
            q, k, v = qkv_project(h, w_qkv[j], g_q[j], g_k[j])
            o = sb_sample(q, k, v, k_cache[j], v_cache[j]) if is_sample else sb_prompt(q, k, v)
            mix = o.reshape(b, t, D_MODEL) @ w_o[j]
            new_k.append(k)
            new_v.append(v)
        else:
            hist = pool_cache[j] if is_sample else jnp.zeros((b, POOL_STATE, D_MODEL), h.dtype)
            mix, st = pool_mixer(h, hist, n_hist, w_pool[j], pool_scale[j])
            new_pool.append(st)
        x = x + gate1 * mix
        h = rms_norm(x, g_ffn[i]) * (1.0 + scale2) + shift2
        x = x + gate2 * swiglu(h, w_gate[i], w_up[i], w_down[i])
    return x, jnp.stack(new_k), jnp.stack(new_v), jnp.stack(new_pool)

def setup_inputs(seed: int = 0) -> dict:
    key = jax.random.key(seed)
    ks = jax.random.split(key, 24)
    f32 = jnp.float32
    nrm = lambda k, shape, s: jax.random.normal(k, shape, f32) * s
    return {
        'x_prompt': nrm(ks[0], (BATCH, SEQ, D_MODEL), 1.0),
        'x_sample': nrm(ks[1], (DEC_BATCH, DEC_SEQ, D_MODEL), 1.0),
        'c_prompt': nrm(ks[2], (BATCH, D_MODEL), 1.0),
        'c_sample': nrm(ks[3], (DEC_BATCH, D_MODEL), 1.0),
        'cache_k': nrm(ks[4], (N_SB_LAYERS, DEC_BATCH, PAST_LEN, N_HEADS, HEAD_DIM), 1.0),
        'cache_v': nrm(ks[5], (N_SB_LAYERS, DEC_BATCH, PAST_LEN, N_HEADS, HEAD_DIM), 1.0),
        'state_pool': nrm(ks[6], (N_POOL_LAYERS, DEC_BATCH, POOL_STATE, D_MODEL), 1.0),
        'w_ada': nrm(ks[7], (DEPTH, D_MODEL, N_MOD * D_MODEL), 0.5 * D_MODEL ** -0.5),
        'b_ada': nrm(ks[8], (DEPTH, N_MOD * D_MODEL), 0.01),
        'g_mix': 1.0 + nrm(ks[9], (DEPTH, D_MODEL), 0.01),
        'g_ffn': 1.0 + nrm(ks[10], (DEPTH, D_MODEL), 0.01),
        'w_qkv': nrm(ks[11], (N_SB_LAYERS, D_MODEL, 3 * D_MODEL), D_MODEL ** -0.5),
        'g_q': 1.0 + nrm(ks[12], (N_SB_LAYERS, HEAD_DIM), 0.01),
        'g_k': 1.0 + nrm(ks[13], (N_SB_LAYERS, HEAD_DIM), 0.01),
        'w_o': nrm(ks[14], (N_SB_LAYERS, D_MODEL, D_MODEL), D_MODEL ** -0.5),
        'w_pool': nrm(ks[15], (N_POOL_LAYERS, N_POOL_GROUPS, POOL_GROUP, POOL_GROUP), POOL_GROUP ** -0.5),
        'pool_scale': 1.0 + nrm(ks[16], (N_POOL_LAYERS, D_MODEL), 0.1),
        'w_gate': nrm(ks[17], (DEPTH, D_MODEL, D_FF), D_MODEL ** -0.5),
        'w_up': nrm(ks[18], (DEPTH, D_MODEL, D_FF), D_MODEL ** -0.5),
        'w_down': nrm(ks[19], (DEPTH, D_FF, D_MODEL), D_FF ** -0.5),
    }

def reference(x_prompt, x_sample, c_prompt, c_sample, cache_k, cache_v, state_pool,
              w_ada, b_ada, g_mix, g_ffn, w_qkv, g_q, g_k, w_o, w_pool, pool_scale,
              w_gate, w_up, w_down):
    y_prompt, k_prompt, v_prompt, pool_prompt = trunk(
        x_prompt, c_prompt, None, None, None, w_ada, b_ada, g_mix, g_ffn, w_qkv, g_q, g_k, w_o,
        w_pool, pool_scale, w_gate, w_up, w_down)
    y_sample, k_sample, v_sample, pool_sample = trunk(
        x_sample, c_sample, cache_k, cache_v, state_pool, w_ada, b_ada, g_mix, g_ffn, w_qkv, g_q, g_k,
        w_o, w_pool, pool_scale, w_gate, w_up, w_down)
    return (y_prompt, y_sample, k_prompt, v_prompt, pool_prompt, k_sample, v_sample, pool_sample)


_drawn_inputs = setup_inputs


def setup_inputs(seed=0):
    import zlib

    import numpy as np

    out = dict(_drawn_inputs(seed))
    spreads = {}
    factors = {'b_ada': 3.338, 'g_mix': 5.613, 'g_ffn': 8.0, 'g_q': 8.0, 'g_k': 5.506}
    for name, (base, spread) in spreads.items():
        noise = np.random.default_rng([zlib.crc32(name.encode()), seed]).standard_normal(out[name].shape)
        drawn = base * np.exp(spread * noise) if base else spread * noise
        out[name] = __import__('jax').numpy.asarray(drawn.astype(out[name].dtype))
    for name, factor in factors.items():
        out[name] = (out[name] * factor).astype(out[name].dtype)
    return out
```

```python
from contextlib import ExitStack, contextmanager

import numpy as np
import concourse.bass as bass
from concourse import mybir

f32 = mybir.dt.float32
f32r = mybir.dt.float32r
ACT = mybir.ActivationFunctionType
ALU = mybir.AluOpType
AX = mybir.AxisListType
ds = bass.ds

P = 128
D = 2048
KT = D // P
NH, HD = 16, 128
PROMPT, STREAMS, STEP = 256, 8, 16
SAMPLE = STREAMS * STEP
TOK = PROMPT + SAMPLE
TT = TOK // P
PAST = 512
PKT = PAST // P
FF = 5632
CHUNKS = FF // 512
NC = 1 + STREAMS
NMOD = 6
MODT = NMOD * D // P
STATE = 15
WINDOWS = (2, 4, 8, 16)
EPS = 1e-6
SCALE = HD ** -0.5
HG = 4

W_ADA = 0
W_QKV = 8
W_O = W_QKV + 7 * HG
W_FFN0 = W_O + 6
W_POOL = W_FFN0 + 5 * CHUNKS
W_FFN1 = W_POOL + 1
W_END = W_FFN1 + 3 * CHUNKS
R_O, R_FFN0, R_POOL = 0, 4, 4 + 4 * CHUNKS
R_FFN1 = R_POOL + 4
R_END = R_FFN1 + 4 * CHUNKS
SHIFT1, SCALE1, GATE1, SHIFT2, SCALE2, GATE2 = (i * KT for i in range(NMOD))
EXT = STATE + PROMPT + STREAMS * (STATE + STEP)
C18 = 2 * NC


class Tally:

    def __init__(self, sem):
        self.sem, self.base, self.n, self.i = sem, 0, 0, None

    def mark(self, instruction):
        instruction.then_inc(self.sem, 1)
        self.n += 1

    def value(self):
        v = self.base + self.n
        if self.i is not None:
            v = (self.i - self.lo) * self.per + v
        return v


@contextmanager
def loop(engine, lo, hi, per):
    with engine.Fori(lo, hi) as i:
        for t, k in per.items():
            t.base, t.n, t.i, t.lo, t.per = t.base + t.n, 0, i, lo, k
        yield i
        for t, k in per.items():
            assert t.n == k, (t.n, k)
            t.base, t.n, t.i = t.base + k * (hi - lo), 0, None


def encoder_step(nc, x_prompt, x_sample, c_prompt, c_sample, cache_k, cache_v, state_pool,
                 w_ada, b_ada, g_mix, g_ffn, w_qkv, g_q, g_k, w_o, w_pool, pool_scale,
                 w_gate, w_up, w_down,
                 y_prompt, y_sample, k_prompt, v_prompt, pool_prompt, k_sample, v_sample,
                 pool_sample):
    ctx = ExitStack()
    with ctx:
        sem_of = {}

        def sem(name):
            sem_of[name] = ctx.enter_context(nc.semaphore(name))
            return sem_of[name]

        q_scratch = nc.dram_tensor("q_scratch", (TOK, D), f32).ap()

        arena_start = (nc.sbuf_base + 31) // 32 * 32
        place = [0]

        def at(offset, name, shape, dt=f32):
            return nc.alloc_sbuf_tensor_at(name, shape, dt, offset=arena_start + offset)

        def nxt(name, shape, dt=f32):
            o = place[0]
            place[0] = (o + int(np.prod(shape[1:])) * 4 + 31) // 32 * 32
            return at(o, name, shape, dt), o

        x, _ = nxt("x", [P, KT, TOK])
        h_hi, H0 = nxt("h_hi", [P, KT, TOK], f32r)
        h_lo, _ = nxt("h_lo", [P, KT, TOK], f32r)
        raw, _ = nxt("raw", [P, 4, 4, 512])
        w_hi, R1 = nxt("w_hi", [P, 4, 4, 512], f32r)
        w_lo, _ = nxt("w_lo", [P, 4, 4, 512], f32r)
        act_f, R2 = nxt("act_f", [P, 4, TOK])
        act_hi, _ = nxt("act_hi", [P, 4, TOK], f32r)
        act_lo, _ = nxt("act_lo", [P, 4, TOK], f32r)
        modT, _ = nxt("modT", [P, 2, MODT, NC])
        par, _ = nxt("par", [P, 2 * MODT + 5 * KT])
        coef, _ = nxt("coef", [P, KT, NC])
        c18, _ = nxt("c18", [P, KT * C18 + 48], f32r)
        ident, _ = nxt("ident", [P, P])
        ones, _ = nxt("ones", [P, P])
        tri, _ = nxt("tri", [P, P])
        mask, _ = nxt("mask", [P, 512])
        fold, _ = nxt("fold", [C18, NC])
        mod18, _ = nxt("mod18", [C18, 512])
        gqk, _ = nxt("gqk", [P, 2, HD])
        rsb, _ = nxt("rsb", [P, TOK])
        tmp_s, _ = nxt("tmp_s", [P, 4, SAMPLE])
        icount, _ = nxt("icount", [P, 4, 16])
        xrow = at(H0, "xrow", [P, TT, D])
        crow = at(H0 + 24576, "crow", [NC, D])
        csil = at(H0 + 32768, "csil", [NC, D])
        prow = at(H0 + 40960, "prow", [96, 3, P])
        yrow = at(H0, "yrow", [P, TT, D])
        nbuf = at(R2, "nbuf", [P, 2, 4, TOK])
        sq = at(R2, "sq", [P, TT, 512])
        qkv_out = at(R2 + 6144, "qkv_out", [P, 2, TT, 512])
        ext = at(R2, "ext", [P, 2, EXT])
        sum_a = at(R2 + 4160, "sum_a", [P, 2, EXT])
        sum_b = at(R2 + 8320, "sum_b", [P, 2, EXT])
        urow = at(R2 + 12480, "urow", [P, 2, 256])
        hrow = at(R2 + 14528, "hrow", [STREAMS * STATE, 2, 256])
        u_dense = at(R2 + 16576, "u_dense", [P, 2, SAMPLE])
        zs_self = at(R2, "zs_self", [P, 4, 512])
        e_buf = at(R2 + 8192, "e_buf", [P, 2, 512])
        sp_buf = at(R2 + 12288, "sp_buf", [P, 2, 512])
        o_new = at(R2 + 16384, "o_new", [P, 4, SAMPLE])
        tok = at(R1, "tok", [P, 3, TT, 512])
        qT = at(R1 + 18432, "qT", [P, 4, TOK])
        kT = at(R1 + 24576, "kT", [P, 4, TOK])
        zs_past = at(R1 + 30720, "zs_past", [P, 4, PKT, STREAMS, STEP])
        later = at(R1 + 38912, "later", [P, 4, PKT, SAMPLE])
        cacheT = at(R1 + 47104, "cacheT", [P, 2, 4, PAST])
        o_f = at(R1 + 63488, "o_f", [P, 4, SAMPLE])

        bank = ctx.enter_context(nc.psum_tensor("bank", [P, 8, 512], f32))

        raw_loaded = [sem(f"raw_loaded{s}") for s in range(4)]
        hi_ready, lo_ready, sub_used = sem("hi_ready"), sem("lo_ready"), sem("sub_used")
        pool_step, const_ready = sem("pool_step"), sem("const_ready")
        x_loaded, c_loaded, par_loaded = sem("x_loaded"), sem("c_loaded"), sem("par_loaded")
        gqk_loaded, silu_c = sem("gqk_loaded"), sem("silu_c")
        xT_done, xT_dve, xT_act = sem("xT_done"), sem("xT_dve"), sem("xT_act")
        cT_done, c18_ready, parT_done, par_ready = sem("cT_done"), sem("c18_ready"), sem("parT_done"), sem("par_ready")
        mod_ready, ada_t, ada_done = sem("mod_ready"), sem("ada_t"), sem("ada_done")
        sq_ready, sq_used, var_ready, std_ready = sem("sq_ready"), sem("sq_used"), sem("var_ready"), sem("std_ready")
        xr_ready, hs_ready, hhi_ready, h_ready = sem("xr_ready"), sem("hs_ready"), sem("hhi_ready"), sem("h_ready")
        dve_step, act_step = sem("dve_step"), sem("act_step")
        qksq_ready, qkvar_ready, qkstd_ready = sem("qksq_ready"), sem("qkvar_ready"), sem("qkstd_ready")
        qk_taken, qk_ready, v_taken = sem("qk_taken"), sem("qk_ready"), sem("v_taken")
        stored = [sem("stored_qv"), sem("stored_k")]
        kv_loaded = [sem(f"kv_loaded{s}") for s in range(4)]
        kv_used, tok_loaded = sem("kv_used"), sem("tok_loaded")
        banks_free, qkT_done, qT_ready, kT_ready = sem("banks_free"), sem("qkT_done"), sem("qT_ready"), sem("kT_ready")
        zself_done, zself_taken = sem("zself_done"), sem("zself_taken")
        cT_act, cT_dve, zpast_done, zpast_taken = sem("cT_act"), sem("cT_dve"), sem("zpast_done"), sem("zpast_taken")
        ln_ready, sp_ready, tri_done, t_ready = sem("ln_ready"), sem("sp_ready"), sem("tri_done"), sem("t_ready")
        w_ready, oself_done, ohi_ready, oself_taken = sem("w_ready"), sem("oself_done"), sem("ohi_ready"), sem("oself_taken")
        later_ready, of_ready, ofhi_ready = sem("later_ready"), sem("of_ready"), sem("ofhi_ready")
        gate_taken, act_f_ready, act_hi_ready, act_ready = sem("gate_taken"), sem("act_f_ready"), sem("act_hi_ready"), sem("act_ready")
        residual_taken = sem("residual_taken")
        hist_loaded = [sem("hist_loaded0"), sem("hist_loaded1")]
        hist_done, hist_taken = sem("hist_done"), sem("hist_taken")
        u_ready, uT_done, uT_taken, pool_stored = sem("u_ready"), sem("uT_done"), sem("uT_taken"), sem("pool_stored")
        dif_ready, difhi_ready, dif_split = sem("dif_ready"), sem("difhi_ready"), sem("dif_split")
        yT_done, y_dve, y_act, y_stored = sem("yT_done"), sem("y_dve"), sem("y_act"), sem("y_stored")

        def rows(w):
            return w.rearrange("(k p) n -> p k n", p=P)

        def ada_src(layer, j, s):
            return rows(w_ada[layer, s * 512:(s + 1) * 512, ds(j * 512, 512)])

        def quads(t, k0, n=4):
            v = t[:, k0:k0 + n, :]
            return v[:, :, 0:PROMPT], v[:, :, PROMPT:TOK].rearrange("p k (b t) -> p k b t", b=STREAMS)

        def per_stream(m, n=4):
            return m[:, :, 1:NC].unsqueeze(3).to_broadcast([P, n, STREAMS, STEP])

        def ext_views(t, n=2):
            s = t[:, 0:n, STATE + PROMPT:EXT].rearrange("p k (b t) -> p k b t", b=STREAMS)
            return t[:, 0:n, STATE:STATE + PROMPT], s[:, :, :, STATE:STATE + STEP], s[:, :, :, 0:STATE]

        parG = par[:, 2 * MODT:]
        c_hi = c18[:, 0:KT * C18].rearrange("p (k c) -> p k c", c=C18)
        hist_rows = state_pool[0].rearrange("b t n -> (b t) n")

        def norm_plan(n):
            layer, ffn = n // 2, n % 2
            return (SCALE2 if ffn else SCALE1), (SHIFT2 if ffn else SHIFT1), KT * (2 * ffn + layer), layer

        def down_bank(s, with_ada):
            return 4 if (s % 2 == 0) == with_ada else 0

        XR, HR = (0, 4, 8, 16), (0, 4, 8, 8)
        STAT_BANK = (5, 2, 4, 4)

        block = ctx.enter_context(nc.Block())

        @block.sync
        def _(sp):
            def load(W, s, src, first=False):
                if not first:
                    sp.wait_ge(lo_ready, 4 * W + s - 3)
                sp.dma_start(raw[:, s], src).then_inc(raw_loaded[s], 16)

            def load_ada(W, layer, j, first=False):
                for s in range(4):
                    load(W, s, ada_src(layer, j, s), first)

            def load_cols(W, w, col):
                for s in range(4):
                    load(W, s, rows(w[s * 512:(s + 1) * 512, ds(col, 512)]))

            load_ada(0, 0, 0, first=True)
            with sp.Fori(1, 8) as j:
                load_ada(j, 0, j)
            with sp.Fori(0, HG) as g:
                W = W_QKV + g * 7
                load_cols(W, w_qkv[0], g * 512)
                load_ada(W + 1, 0, g * 4 + 8)
                load_cols(W + 2, w_qkv[0], g * 512 + D)
                load_ada(W + 3, 0, g * 4 + 9)
                load_cols(W + 4, w_qkv[0], g * 512 + 2 * D)
                load_ada(W + 5, 0, g * 4 + 10)
                load_ada(W + 6, 0, g * 4 + 11)

            def load_cache(col, j, ahead=0):
                src = (cache_k if j < 8 else cache_v)[0, j % 8].rearrange("(k p) h d -> p k (h d)", p=P)
                sp.dma_start(raw[:, j % 4], src[:, :, ahead:][:, :, ds(col, 512)]).then_inc(kv_loaded[j % 4], 16)

            def load_tok(col, ahead=0):
                cols = ds(col, 512)
                flat = "b t h d -> (b t) (h d)"
                sp.dma_start(tok[:, 0], q_scratch[:, ahead:][:, cols].rearrange("(t p) n -> p t n", p=P)).then_inc(tok_loaded, 16)
                for i, (a, b) in ((1, (k_prompt, k_sample)), (2, (v_prompt, v_sample))):
                    sp.dma_start(tok[:, i, 0:2], a[0].rearrange(flat)[:, ahead:][:, cols].rearrange("(t p) n -> p t n", p=P)).then_inc(tok_loaded, 16)
                    sp.dma_start(tok[:, i, 2], b[0].rearrange(flat)[:, ahead:][:, cols]).then_inc(tok_loaded, 16)

            def cache_rest(g, col):
                for j in range(4, 16):
                    if j != 8:
                        sp.wait_ge(kv_used, 16 * g + (5 if j == 7 else j - 3))
                    load_cache(col, j)

            for s in range(4):
                sp.wait_ge(lo_ready, 4 * (W_O - 1) + s + 1)
                load_cache(0, s)
            sp.wait_ge(sub_used, 4 * W_O)
            sp.wait_ge(stored[0], 16 * 4 * HG)
            sp.wait_ge(stored[1], 16 * 2 * HG)
            load_tok(0)
            with sp.Fori(0, HG - 1) as g:
                col = sp.snap(g * 512)
                cache_rest(g, col)
                load_tok(col, 512)
                for j in range(4):
                    sp.wait_ge(kv_used, 16 * g + 13 + j)
                    load_cache(col, j, 512)
            cache_rest(HG - 1, 512 * (HG - 1))

            for i in range(2):
                for b in range(2):
                    for s in range(4):
                        if i == 0 and b == 0:
                            sp.wait_ge(kv_used, 16 * HG - 3 + s)
                            sp.dma_start(raw[:, s], rows(w_o[0, s * 512:(s + 1) * 512, 0:512])).then_inc(raw_loaded[s], 16)
                        else:
                            c = (2 * i + b) * 512
                            load(W_O + 3 * i + b, s, rows(w_o[0, s * 512:(s + 1) * 512, c:c + 512]))
                load_ada(W_O + 3 * i + 2, 1, i)

            def load_down(W, layer, c):
                for s in range(4):
                    load(W, s, rows(w_down[layer, ds(c * 512, 512), s * 512:(s + 1) * 512]))

            with sp.Fori(0, CHUNKS) as c:
                W = W_FFN0 + c * 5
                load_cols(W, w_gate[0], c * 512)
                load_cols(W + 1, w_up[0], c * 512)
                load_ada(W + 2, 1, c * 2 + 2)
                load_ada(W + 3, 1, c * 2 + 3)
                load_down(W + 4, 0, c)
            for s in range(4):
                load(W_POOL, s, rows(w_pool[0, s]))
            load_cols(W_FFN1, w_gate[1], 0)
            for j in range(8):
                sp.wait_ge(uT_taken, j + 1)
                cols = slice(256 * j, 256 * j + 256)
                sp.dma_start(pool_prompt[0, 0, :, cols], urow[P - STATE:P, 0, :]).then_inc(pool_stored, 16)
                for b in range(STREAMS):
                    sp.dma_start(pool_sample[0, b, :, cols],
                                 urow[STEP * b + 1:STEP * (b + 1), 1, :]).then_inc(pool_stored, 16)
            load_cols(W_FFN1 + 1, w_up[1], 0)
            load_down(W_FFN1 + 2, 1, 0)
            with sp.Fori(1, CHUNKS) as c:
                W = W_FFN1 + c * 3
                load_cols(W, w_gate[1], c * 512)
                load_cols(W + 1, w_up[1], c * 512)
                load_down(W + 2, 1, c)
            sp.wait_ge(pool_stored, 16 * 9 * 8)
            sp.wait_ge(y_act, 6)
            sp.wait_ge(y_dve, 6)
            for t in range(TT):
                dst = y_prompt[0, t * P:(t + 1) * P] if t < 2 else y_sample.rearrange("b t n -> (b t) n")
                sp.dma_start(dst, yrow[:, t]).then_inc(y_stored, 16)
            sp.wait_ge(y_stored, 16 * TT)

        @block.gpsimd
        def _(pool):
            step = Tally(pool_step)

            def do(ins):
                step.mark(ins)
                pool.wait_ge(pool_step, step.value())

            do(pool.memset(ident[:], 0.0))
            do(pool.affine_select(out=ident[:], in_=ident[:], compare_op=ALU.not_equal, fill=1.0, base=0,
                                  pattern=[[-1, P]], channel_multiplier=1))
            do(pool.memset(ones[:], 1.0))
            do(pool.affine_select(out=tri[:], in_=ones[:], compare_op=ALU.is_ge, fill=0.0, base=0,
                                  pattern=[[-1, P]], channel_multiplier=1))
            do(pool.memset(mask[:], 3e38))
            for c0, n in ((0, 256), (256, 128), (384, 128)):
                part = mask[:, c0:c0 + n]
                do(pool.affine_select(out=part, in_=part, compare_op=ALU.is_gt, fill=-1e30, base=0,
                                      pattern=[[1, n]], channel_multiplier=-1))
            part = mask[:, 384:512].rearrange("p (b t) -> p b t", b=STREAMS)
            do(pool.affine_select(out=part, in_=part, compare_op=ALU.is_ge, fill=-1e30, base=0,
                                  pattern=[[-STEP, STREAMS], [0, STEP]], channel_multiplier=1))
            do(pool.memset(fold[:], 0.0))
            for off in (0, NC):
                do(pool.affine_select(out=fold[:], in_=fold[:], compare_op=ALU.not_equal, fill=1.0, base=-off,
                                      pattern=[[-1, NC]], channel_multiplier=1))
            for i in range(4):
                do(pool.iota(icount[:, i, :], pattern=[[1, 16]], base=1, channel_multiplier=0,
                             allow_small_or_imprecise_dtypes=True))
            pool.memset(tmp_s[:, 0, 0:1], 0.0).then_inc(const_ready, 1)

        @block.scalar
        def _(act):
            step = Tally(act_step)

            def hi(W, subs, first=False):
                for s in subs:
                    act.wait_ge(raw_loaded[s], 16 * W + 16)
                    if not first:
                        act.wait_ge(sub_used, 4 * W + s - 3)
                    act.activation(w_hi[:, s], raw[:, s], ACT.Copy).then_inc(hi_ready, 1)

            def mod_out(W, a, acc_bank, first=False):
                act.wait_ge(sub_used, 4 * W + 4)
                if not first:
                    act.wait_ge(ada_t, a)
                act.activation(mod18[:], bank[0:C18, acc_bank, :], ACT.Copy).then_inc(mod_ready, 1)

            def norm_stats(n):
                for g in range(4):
                    if n == 0:
                        act.wait_ge(xT_dve, 6)
                        act.wait_ge(xT_act, 6)
                    else:
                        act.wait_ge(residual_taken, (R_FFN0, R_POOL, R_FFN1)[n - 1] - 3 + g)
                    if n >= 2:
                        act.wait_ge(sub_used, 4 * (W_POOL, W_FFN1)[n - 2])
                    if g >= 2:
                        act.wait_ge(sq_used, 4 * n + g - 1)
                    act.activation(nbuf[:, g % 2], x[:, 4 * g:4 * g + 4, :], ACT.Square).then_inc(sq_ready, 1)
                act.wait_ge(var_ready, n + 1)
                act.activation(rsb[:], rsb[:], ACT.Sqrt).then_inc(std_ready, 1)

            def norm_apply(n):
                _, shift, _, layer = norm_plan(n)
                for g in range(4):
                    act.wait_ge(xr_ready, XR[n] + g + 1)
                    for k in range(4):
                        v = nbuf[:, g % 2, k, 0:PROMPT]
                        m = 4 * g + k
                        step.mark(act.activation(v, v, ACT.Identity, bias=modT[:, layer, shift + m, 0:1],
                                                 scale=coef[:, m, 0:1]))
                    act.wait_ge(act_step, step.value())
                    act.wait_ge(hs_ready, XR[n] + g + 1)
                    act.activation(h_hi[:, 4 * g:4 * g + 4, :], nbuf[:, g % 2], ACT.Copy).then_inc(hhi_ready, 1)

            act.dma_start(crow[0:1], c_prompt).then_inc(c_loaded, 16)
            act.dma_start(crow[1:NC], c_sample).then_inc(c_loaded, 16)
            for t in range(TT):
                src = x_prompt[0, t * P:(t + 1) * P] if t < 2 else x_sample.rearrange("b t n -> (b t) n")
                act.dma_start(xrow[:, t], src).then_inc(x_loaded, 16)
            for i in range(2):
                act.dma_start(prow[:, i], b_ada[i].rearrange("(a n) -> a n", n=P)).then_inc(par_loaded, 16)
            for i, g in enumerate((g_mix, g_ffn)):
                for l in range(2):
                    r = KT * (2 * i + l)
                    act.dma_start(prow[r:r + KT, 2], g[l].rearrange("(a n) -> a n", n=P)).then_inc(par_loaded, 16)
            act.dma_start(prow[4 * KT:5 * KT, 2], pool_scale[0].rearrange("(a n) -> a n", n=P)).then_inc(par_loaded, 16)
            for i, g in enumerate((g_q, g_k)):
                act.dma_start(gqk[:, i], g[0:1, :].to_broadcast([P, HD])).then_inc(gqk_loaded, 16)

            act.wait_ge(c_loaded, 32)
            act.activation(csil[:], crow[:], ACT.Silu).then_inc(silu_c, 1)
            hi(0, range(4), first=True)
            for i in range(1, 12, 2):
                t, q = i // 4, i % 4
                act.wait_ge(xT_done, i + 1)
                act.activation(x[:, 4 * q:4 * q + 4, t * P:(t + 1) * P],
                               bank[:, i % 6].rearrange("p (k c) -> p k c", k=4), ACT.Copy).then_inc(xT_act, 1)
            hi(1, range(3))
            mod_out(0, 0, 6, first=True)
            hi(1, [3])
            with act.Fori(1, 8) as a:
                hi(a + 1, range(3))
                mod_out(a, a, 6)
                hi(a + 1, [3])
            norm_stats(0)
            norm_apply(0)

            def square_heads(g, i):
                W = W_QKV + 7 * g + 2 * i
                act.wait_ge(sub_used, 4 * W + 4)
                b0 = 3 * i
                act.activation(sq[:], bank[:, b0:b0 + 3, :], ACT.Square).then_inc(qksq_ready, 1)
                act.wait_ge(qkvar_ready, 2 * g + i + 1)
                act.activation(rsb[:, 12 * i:12 * i + 12], rsb[:, 12 * i:12 * i + 12], ACT.Sqrt).then_inc(qkstd_ready, 1)

            def store(g, i):
                flat = "b t h d -> (b t) (h d)"
                cols = ds(g * 512, 512)
                slot = (0, 1, 0)[i]
                a, b = ((q_scratch[0:PROMPT], q_scratch[PROMPT:TOK]),
                        (k_prompt[0].rearrange(flat), k_sample[0].rearrange(flat)),
                        (v_prompt[0].rearrange(flat), v_sample[0].rearrange(flat)))[i]
                if i < 2:
                    act.wait_ge(qk_ready, 2 * g + i + 1)
                else:
                    act.wait_ge(v_taken, g + 1)
                act.dma_start(a[:, cols].rearrange("(t p) n -> p t n", p=P), qkv_out[:, slot, 0:2]).then_inc(stored[slot], 16)
                act.dma_start(b[:, cols], qkv_out[:, slot, 2]).then_inc(stored[slot], 16)

            def qkv_group(g, last):
                W = W_QKV + 7 * g
                a = 8 + 4 * g
                hi(W + 1, range(3)); square_heads(g, 0); hi(W + 1, [3])
                hi(W + 2, range(3)); mod_out(W + 1, a, 6); store(g, 0); hi(W + 2, [3])
                hi(W + 3, range(3)); square_heads(g, 1); hi(W + 3, [3])
                hi(W + 4, range(3)); mod_out(W + 3, a + 1, 6); store(g, 1); hi(W + 4, [3])
                hi(W + 5, range(3))
                act.wait_ge(sub_used, 4 * W + 20)
                act.wait_ge(stored[0], 64 * g + 32)
                act.activation(qkv_out[:, 0], bank[:, 0:3, :], ACT.Copy).then_inc(v_taken, 1)
                hi(W + 5, [3])
                hi(W + 6, range(3)); mod_out(W + 5, a + 2, 6); store(g, 2); hi(W + 6, [3])
                if not last:
                    hi(W + 7, range(3)); mod_out(W + 6, a + 3, 6); hi(W + 7, [3])
                else:
                    mod_out(W + 6, a + 3, 6)

            with act.Fori(0, HG - 1) as g:
                qkv_group(g, False)
            qkv_group(HG - 1, True)

            def softplus_rest(z, n):
                step.mark(act.activation(e_buf[:], z, ACT.Abs))
                act.wait_ge(act_step, step.value())
                step.mark(act.activation(e_buf[:], e_buf[:], ACT.Exp, scale=-1.0))
                act.wait_ge(act_step, step.value())
                act.activation(e_buf[:], e_buf[:], ACT.Ln, bias=1.0).then_inc(ln_ready, 1)

            with loop(act, 0, HG, {step: 8}) as g:
                act.wait_ge(qkT_done, g + 1)
                act.activation(qT[:], bank[:, 0:4, 0:TOK], ACT.Copy).then_inc(qT_ready, 1)

                def cache_out(b):
                    act.wait_ge(kv_used, 16 * g + b + 1)
                    act.activation(cacheT[:, b % 2, 0:2, :], bank[:, 4:6, :], ACT.Copy).then_inc(cT_act, 1)

                def self_rest(p):
                    act.wait_ge(zself_taken, g + 1)
                    if p:
                        act.wait_ge(sp_ready, 4 * g + 1)
                    softplus_rest(zs_self[:, 2 * p:2 * p + 2], None)

                def self_w(p):
                    act.wait_ge(t_ready, 4 * g + p + 1)
                    v = zs_self[:, 2 * p:2 * p + 2]
                    act.activation(v, v, ACT.Exp).then_inc(w_ready, 1)

                def self_hi(p):
                    act.wait_ge(oself_done, 2 * g + p + 1)
                    act.activation(h_hi[:, ds(g * 4 + 2 * p, 2), 0:PROMPT], bank[:, 2:4, 0:PROMPT], ACT.Copy).then_inc(ohi_ready, 1)

                cache_out(0)
                self_rest(0)
                cache_out(1); cache_out(2); cache_out(3)
                self_w(0)
                self_rest(1)
                cache_out(4); cache_out(5)
                self_hi(0)
                cache_out(6)
                cache_out(7)
                self_w(1)
                self_hi(1)
                for p in range(2):
                    act.wait_ge(zpast_taken, 8 * g + 8)
                    act.wait_ge(sp_ready, 4 * g + 2 + p)
                    softplus_rest(zs_past[:, 2 * p:2 * p + 2].rearrange("p h k b t -> p h (k b t)"), None)
                for p in range(2):
                    act.wait_ge(t_ready, 4 * g + 3 + p)
                    v = zs_past[:, 2 * p:2 * p + 2].rearrange("p h k b t -> p h (k b t)")
                    act.activation(v, v, ACT.Exp).then_inc(w_ready, 1)
                act.wait_ge(of_ready, g + 1)
                act.activation(h_hi[:, ds(g * 4, 4), PROMPT:TOK], o_f[:], ACT.Copy).then_inc(ofhi_ready, 1)

            act.wait_ge(banks_free, HG + 1)
            hi(W_O, range(4))
            for i in range(2):
                W = W_O + 3 * i
                hi(W + 1, range(4))
                hi(W + 2, range(4))
                hi(W + 3, range(3)); mod_out(W + 2, 24 + i, 0); hi(W + 3, [3])
            norm_stats(1)
            norm_apply(1)

            def ffn_chunk(W, c, with_ada, last=False):
                hi(W + 1, range(3))
                act.wait_ge(sub_used, 4 * W + 4)
                act.activation(act_f[:], bank[:, 0:4, 0:TOK], ACT.Silu).then_inc(gate_taken, 1)
                hi(W + 1, [3])
                hi(W + 2, range(3))
                for m in range(4):
                    act.wait_ge(act_f_ready, 4 * c + m + 1)
                    act.activation(act_hi[:, m], act_f[:, m], ACT.Copy).then_inc(act_hi_ready, 1)
                hi(W + 2, [3])
                if with_ada:
                    a = 26 + 2 * c
                    hi(W + 3, range(3)); mod_out(W + 2, a, 0); hi(W + 3, [3])
                    hi(W + 4, range(3)); mod_out(W + 3, a + 1, 1); hi(W + 4, [3])
                    hi(W + 5, range(4))
                elif not last:
                    hi(W + 3, range(4))

            with act.Fori(0, CHUNKS) as c:
                ffn_chunk(W_FFN0 + c * 5, c, True)

            norm_stats(2)

            def load_hist(j):
                if j >= 2:
                    act.wait_ge(hist_done, j - 1)
                act.dma_start(hrow[:, j % 2], hist_rows[:, 256 * j:256 * j + 256]).then_inc(hist_loaded[j % 2], 16)

            load_hist(0)
            load_hist(1)
            for j in range(8):
                act.wait_ge(hist_done, j + 1)
                hist = ext_views(ext)[2]
                act.wait_ge(xr_ready, XR[2] + j + 1)
                act.activation(hist, bank[:, 1, 0:240].rearrange("p (k b t) -> p k b t", k=2, b=STREAMS),
                               ACT.Copy).then_inc(hist_taken, 1)
                for k in range(2):
                    m = 2 * j + k
                    v = ext[:, k, STATE:STATE + PROMPT]
                    step.mark(act.activation(v, v, ACT.Identity, bias=modT[:, 1, SHIFT1 + m, 0:1], scale=coef[:, m, 0:1]))
                act.wait_ge(hs_ready, XR[2] + j + 1)
                act.activation(u_dense[:].rearrange("p k (b t) -> p k b t", b=STREAMS), ext_views(ext)[1], ACT.Copy).then_inc(u_ready, 1)
                if j + 2 < 8:
                    load_hist(j + 2)
                act.wait_ge(uT_done, j + 1)
                if j:
                    act.wait_ge(pool_stored, 144 * j)
                act.activation(urow[:], bank[:, 0, :].rearrange("p (t n) -> p t n", t=2), ACT.Copy).then_inc(uT_taken, 1)
                act.wait_ge(dif_ready, j + 1)
                dif = (sum_b, sum_a, sum_b, sum_a)[j // 2]
                act.activation(h_hi[:, 2 * j:2 * j + 2, :], dif[:, :, 0:TOK], ACT.Copy).then_inc(difhi_ready, 1)
                if j >= 3 and j % 2:
                    hi(W_FFN1, [j // 2 - 1])
            hi(W_FFN1, [3])
            norm_stats(3)
            norm_apply(3)

            with act.Fori(0, CHUNKS - 1) as c:
                ffn_chunk(W_FFN1 + c * 3, c + CHUNKS, False)
            ffn_chunk(W_FFN1 + 3 * (CHUNKS - 1), 2 * CHUNKS - 1, False, last=True)

            for i in range(1, 12, 2):
                t, q = i % TT, i // TT
                act.wait_ge(yT_done, i + 1)
                act.activation(yrow[:, t, q * 512:(q + 1) * 512], bank[:, i % 6], ACT.Copy).then_inc(y_act, 1)

        @block.vector
        def _(dve):
            step = Tally(dve_step)

            def own():
                dve.wait_ge(dve_step, step.value())

            def lo(W, subs):
                for s in subs:
                    dve.wait_ge(hi_ready, 4 * W + s + 1)
                    dve.tensor_tensor(w_lo[:, s], raw[:, s], w_hi[:, s].bitcast(f32), ALU.subtract).then_inc(lo_ready, 1)

            def mod_in(a, layer, j, t_bank):
                dve.wait_ge(ada_t, a + 1)
                bias = par[:, ds(MODT * layer + 4 * j, 4)].unsqueeze(2).to_broadcast([P, 4, NC])
                dve.tensor_tensor(modT[:, layer, ds(4 * j, 4), :],
                                  bank[:, t_bank, 0:4 * NC].rearrange("p (k c) -> p k c", k=4),
                                  bias, ALU.add).then_inc(ada_done, 1)

            def norm_root(n):
                scale, _, gain, layer = norm_plan(n)
                stat_bank = STAT_BANK[n]
                dve.wait_ge(ada_done, (8, 24, 48, 48)[n])
                step.mark(dve.scalar_tensor_tensor(coef[:], modT[:, layer, scale:scale + KT, :], 1.0,
                                                   parG[:, gain:gain + KT].unsqueeze(2).to_broadcast([P, KT, NC]),
                                                   ALU.add, ALU.mult))
                dve.wait_ge(sq_used, 4 * n + 4)
                dve.tensor_scalar(rsb[:], bank[:, stat_bank, 0:TOK], 1.0 / D, EPS, ALU.mult, ALU.add).then_inc(var_ready, 1)
                dve.wait_ge(std_ready, n + 1)
                step.mark(dve.reciprocal(rsb[:], rsb[:]))
                own()

            def norm_apply(n):
                _, shift, _, layer = norm_plan(n)
                for g in range(5):
                    if g < 4:
                        if g >= 2:
                            dve.wait_ge(h_ready, HR[n] + g - 1)
                        nb = nbuf[:, g % 2]
                        dve.tensor_tensor(nb, x[:, 4 * g:4 * g + 4, :], rsb[:].unsqueeze(1).to_broadcast([P, 4, TOK]),
                                          ALU.mult).then_inc(xr_ready, 1)
                        dve.wait_ge(xr_ready, XR[n] + g + 1)
                        s = nb[:, :, PROMPT:TOK].rearrange("p k (b t) -> p k b t", b=STREAMS)
                        step.mark(dve.tensor_tensor(s, s, per_stream(coef[:, 4 * g:4 * g + 4, :]), ALU.mult))
                        own()
                        m = shift + 4 * g
                        dve.tensor_tensor(s, s, per_stream(modT[:, layer, m:m + 4, :]), ALU.add).then_inc(hs_ready, 1)
                    if g:
                        dve.wait_ge(hhi_ready, HR[n] + g)
                        q = 4 * (g - 1)
                        dve.tensor_tensor(h_lo[:, q:q + 4, :], nbuf[:, (g - 1) % 2], h_hi[:, q:q + 4, :].bitcast(f32),
                                          ALU.subtract).then_inc(h_ready, 1)

            def add_quad(b0, m0, layer, gate):
                ps = bank[:, b0:b0 + 4, 0:TOK]
                mod = modT[:, layer, gate + m0:gate + m0 + 4, :]
                step.mark(dve.tensor_tensor(tmp_s[:].rearrange("p k (b t) -> p k b t", b=STREAMS),
                                            ps[:, :, PROMPT:TOK].rearrange("p k (b t) -> p k b t", b=STREAMS),
                                            per_stream(mod), ALU.mult))
                for k in range(4):
                    xv = x[:, m0 + k, 0:PROMPT]
                    step.mark(dve.scalar_tensor_tensor(xv, ps[:, k, 0:PROMPT], mod[:, k, 0:1], xv, ALU.mult, ALU.add))
                own()
                xs = x[:, m0:m0 + 4, PROMPT:TOK]
                dve.tensor_tensor(xs, xs, tmp_s[:], ALU.add).then_inc(residual_taken, 1)
            ADD = 5

            dve.memset(c18[:, KT * C18:].bitcast(f32), 0.0).then_inc(c18_ready, 1)
            dve.wait_ge(const_ready, 1)
            for i, w in enumerate(WINDOWS):
                step.mark(dve.tensor_scalar(icount[:, i], icount[:, i], float(w), None, ALU.min))
            own()
            step.mark(dve.reciprocal(icount[:], icount[:]))
            dve.wait_ge(cT_done, 1)
            cT = bank[:, 6, 0:KT * NC].rearrange("p (k c) -> p k c", c=NC)
            dve.tensor_copy(c_hi[:, :, 0:NC], cT).then_inc(c18_ready, 1)
            dve.wait_ge(c18_ready, 2)
            dve.tensor_tensor(c_hi[:, :, NC:C18], cT, c_hi[:, :, 0:NC].bitcast(f32), ALU.subtract).then_inc(c18_ready, 1)
            dve.wait_ge(parT_done, 1)
            dve.tensor_copy(par[:], bank[:, 7, 0:2 * MODT + 5 * KT]).then_inc(par_ready, 1)
            lo(0, range(4))
            for i in range(0, 12, 2):
                t, q = i // 4, i % 4
                dve.wait_ge(xT_done, i + 1)
                dve.tensor_copy(x[:, 4 * q:4 * q + 4, t * P:(t + 1) * P],
                                bank[:, i % 6].rearrange("p (k c) -> p k c", k=4)).then_inc(xT_dve, 1)
            dve.wait_ge(par_ready, 1)
            with loop(dve, 0, 8, {}) as a:
                lo(a + 1, range(3))
                mod_in(a, 0, a, 7)
                lo(a + 1, [3])
            norm_root(0)
            norm_apply(0)
            dve.wait_ge(gqk_loaded, 32)

            def norm_heads(g, i):
                b0 = 3 * i
                r = rsb[:, 12 * i:12 * i + 12]
                ps = bank[:, b0:b0 + 3, :].rearrange("p t (h d) -> p t h d", d=HD)
                out = qkv_out[:, i].rearrange("p t (h d) -> p t h d", d=HD)
                dve.wait_ge(qksq_ready, 2 * g + i + 1)
                step.mark(dve.tensor_reduce(r.rearrange("p (t h) -> p t h", t=3), sq[:].rearrange("p t (h d) -> p t h d", d=HD), AX.X, ALU.add))
                own()
                dve.tensor_scalar(r, r, 1.0 / HD, EPS, ALU.mult, ALU.add).then_inc(qkvar_ready, 1)
                gain = gqk[:, i].unsqueeze(1).unsqueeze(1).to_broadcast([P, TT, 4, HD])
                dve.tensor_tensor(out, ps, gain, ALU.mult).then_inc(qk_taken, 1)
                dve.wait_ge(qkstd_ready, 2 * g + i + 1)
                step.mark(dve.reciprocal(r, r))
                own()
                dve.wait_ge(qk_taken, 2 * g + i + 1)
                dve.tensor_tensor(out, out, r.rearrange("p (t h) -> p t h", t=3).unsqueeze(3).to_broadcast([P, TT, 4, HD]),
                                  ALU.mult).then_inc(qk_ready, 1)

            def qkv_group(g, first, last):
                W = W_QKV + 7 * g
                a = 8 + 4 * g
                lo(W + 1, range(3))
                if not first:
                    dve.wait_ge(stored[0], 64 * g)
                norm_heads(g, 0)
                lo(W + 1, [3])
                lo(W + 2, range(4))
                lo(W + 3, range(3))
                if not first:
                    dve.wait_ge(stored[1], 32 * g)
                norm_heads(g, 1)
                mod_in(a, 0, a, 7)
                lo(W + 3, [3])
                lo(W + 4, range(4))
                lo(W + 5, range(3)); mod_in(a + 1, 0, a + 1, 7); lo(W + 5, [3])
                lo(W + 6, range(3)); mod_in(a + 2, 0, a + 2, 7); lo(W + 6, [3])
                if not last:
                    lo(W + 7, range(3)); mod_in(a + 3, 0, a + 3, 7); lo(W + 7, [3])
                else:
                    mod_in(a + 3, 0, a + 3, 7)

            qkv_group(0, True, False)
            with loop(dve, 1, HG - 1, {step: 4}) as g:
                qkv_group(g, False, False)
            qkv_group(HG - 1, False, True)

            dve.wait_ge(v_taken, HG)
            dve.wait_ge(mod_ready, 24)
            dve.wait_ge(const_ready, 1)
            dve.memset(tmp_s[:, 0, 0:1], 0.0).then_inc(banks_free, 1)

            with loop(dve, 0, HG, {step: 8}) as g:
                dve.wait_ge(qkT_done, g + 1)
                dve.tensor_copy(kT[:], bank[:, 4:8, 0:TOK]).then_inc(kT_ready, 1)
                dve.wait_ge(zself_done, g + 1)
                dve.scalar_tensor_tensor(zs_self[:], bank[:, 0:4, :], SCALE, mask[:].unsqueeze(1).to_broadcast([P, 4, 512]),
                                         ALU.mult, ALU.min).then_inc(zself_taken, 1)

                def cache_out(b):
                    dve.wait_ge(kv_used, 16 * g + b + 1)
                    dve.tensor_copy(cacheT[:, b % 2, 2:4, :], bank[:, 6:8, :]).then_inc(cT_dve, 1)

                def scores_out(b):
                    dve.wait_ge(zpast_done, 8 * g + b + 1)
                    dve.tensor_scalar(zs_past[:, :, :, b, :], bank[:, b % 2, 0:256].rearrange("p (h k t) -> p h k t", h=4, k=PKT),
                                      SCALE, None, ALU.mult).then_inc(zpast_taken, 1)

                def self_sp(p):
                    dve.wait_ge(ln_ready, 4 * g + p + 1)
                    if p:
                        dve.wait_ge(tri_done, 4 * g + 1)
                        own()
                    dve.scalar_tensor_tensor(sp_buf[:], zs_self[:, 2 * p:2 * p + 2], 0.0, e_buf[:], ALU.max, ALU.add).then_inc(sp_ready, 1)
                    dve.wait_ge(sp_ready, 4 * g + p + 1)
                    step.mark(dve.tensor_copy(later[:, 2 * p:2 * p + 2, PKT - 1, :], sp_buf[:, :, 384:512]))

                def self_t(p):
                    dve.wait_ge(tri_done, 4 * g + p + 1)
                    v = zs_self[:, 2 * p:2 * p + 2]
                    dve.tensor_tensor(v, v, bank[:, 2:4, :], ALU.subtract).then_inc(t_ready, 1)

                def self_out(p):
                    dve.wait_ge(oself_done, 2 * g + p + 1)
                    dve.wait_ge(ohi_ready, 2 * g + p + 1)
                    step.mark(dve.tensor_copy(o_new[:, 2 * p:2 * p + 2, :], bank[:, 2:4, PROMPT:TOK]))
                    k = ds(g * 4 + 2 * p, 2)
                    dve.tensor_tensor(h_lo[:, k, 0:PROMPT], bank[:, 2:4, 0:PROMPT], h_hi[:, k, 0:PROMPT].bitcast(f32),
                                      ALU.subtract).then_inc(oself_taken, 1)

                cache_out(0)
                cache_out(1); scores_out(0)
                self_sp(0)
                cache_out(2); scores_out(1)
                cache_out(3); scores_out(2)
                self_t(0)
                cache_out(4); scores_out(3)
                self_sp(1)
                cache_out(5); scores_out(4)
                self_out(0)
                cache_out(6); scores_out(5)
                cache_out(7); scores_out(6)
                self_t(1)
                scores_out(7)
                self_out(1)
                for p in range(2):
                    pair = slice(2 * p, 2 * p + 2)
                    z = zs_past[:, pair].rearrange("p h k b t -> p h (k b t)")
                    dve.wait_ge(ln_ready, 4 * g + 3 + p)
                    dve.wait_ge(tri_done, 4 * g + 2 + p)
                    own()
                    dve.scalar_tensor_tensor(sp_buf[:], z, 0.0, e_buf[:], ALU.max, ALU.add).then_inc(sp_ready, 1)
                    dve.wait_ge(sp_ready, 4 * g + 3 + p)
                    for k in (2, 1, 0):
                        ins = dve.tensor_tensor(later[:, pair, k, :], later[:, pair, k + 1, :],
                                                sp_buf[:, :, (k + 1) * P:(k + 2) * P], ALU.add)
                        if k:
                            step.mark(ins)
                            own()
                        else:
                            ins.then_inc(later_ready, 1)
                    dve.wait_ge(tri_done, 4 * g + 3 + p)
                    dve.tensor_tensor(z, z, bank[:, 2:4, :], ALU.subtract).then_inc(t_ready, 1)
                dve.wait_ge(kv_used, 16 * g + 16)
                dve.wait_ge(oself_taken, 2 * g + 2)
                dve.tensor_tensor(o_f[:], bank[:, 4, :].rearrange("p (h t) -> p h t", h=4), o_new[:], ALU.add).then_inc(of_ready, 1)
                dve.wait_ge(ofhi_ready, g + 1)
                k = ds(g * 4, 4)
                dve.tensor_tensor(h_lo[:, k, PROMPT:TOK], o_f[:], h_hi[:, k, PROMPT:TOK].bitcast(f32), ALU.subtract).then_inc(banks_free, 1)

            own()
            lo(W_O, range(4))
            for i in range(2):
                W = W_O + 3 * i
                for b in range(2):
                    lo(W + 1 + b, range(3))
                    dve.wait_ge(sub_used, 4 * (W + b) + 4)
                    if i or b:
                        dve.wait_ge(residual_taken, 2 * i + b)
                    add_quad(4 * b, 4 * (2 * i + b), 0, GATE1)
                    lo(W + 1 + b, [3])
                lo(W + 3, range(3)); mod_in(24 + i, 1, i, 1); lo(W + 3, [3])
            norm_root(1)
            norm_apply(1)

            def ffn_chunk(W, c, layer, r, with_ada, last=False):
                lo(W + 1, range(4))
                lo(W + 2, range(3))
                dve.wait_ge(sub_used, 4 * W + 8)
                dve.wait_ge(gate_taken, c + 1)

                def split_act(m):
                    dve.wait_ge(act_hi_ready, 4 * c + m + 1)
                    dve.tensor_tensor(act_lo[:, m], act_f[:, m], act_hi[:, m].bitcast(f32), ALU.subtract).then_inc(act_ready, 1)

                for m in range(4):
                    dve.tensor_tensor(act_f[:, m], act_f[:, m], bank[:, 4 + m, 0:TOK], ALU.mult).then_inc(act_f_ready, 1)
                    if m:
                        split_act(m - 1)
                split_act(3)
                lo(W + 2, [3])
                down = W + 2
                if with_ada:
                    a, j = 26 + 2 * c, 2 * c + 2
                    down = W + 4
                    lo(W + 3, range(4))
                    lo(W + 4, range(3)); mod_in(a, 1, j, 2); lo(W + 4, [3])
                for s in range(4):
                    if not last:
                        lo(down + 1, [s])
                    dve.wait_ge(sub_used, 4 * down + s + 1)
                    dve.wait_ge(residual_taken, r + s)
                    add_quad(down_bank(s, with_ada), 4 * s, layer, GATE2)
                    if with_ada and s == 0:
                        mod_in(a + 1, 1, j + 1, 3)

            with loop(dve, 0, CHUNKS, {step: 4 * ADD}) as c:
                ffn_chunk(W_FFN0 + c * 5, c, 0, R_FFN0 + c * 4, True)

            norm_root(2)
            gate = modT[:, 1, GATE1:GATE1 + KT, :]
            step.mark(dve.tensor_tensor(gate, gate, parG[:, 4 * KT:5 * KT].unsqueeze(2).to_broadcast([P, KT, NC]), ALU.mult))
            def pooled(s):
                lo(W_FFN1, [s])
                dve.wait_ge(sub_used, 4 * W_POOL + s + 1)
                dve.wait_ge(residual_taken, R_POOL + s)
                add_quad(4, 4 * s, 1, GATE1)

            u_p, u_s, _ = ext_views(ext)
            for j in range(8):
                g, w = j // 2, WINDOWS[j // 2]
                own()
                if j:
                    dve.wait_ge(dif_split, j)
                    dve.wait_ge(uT_done, j)
                xp, xs = quads(x, 2 * j, 2)
                step.mark(dve.memset(ext[:, :, 0:STATE], 0.0))
                step.mark(dve.tensor_tensor(u_p, xp, rsb[:, 0:PROMPT].unsqueeze(1).to_broadcast([P, 2, PROMPT]), ALU.mult))
                rs_s = rsb[:, PROMPT:TOK].rearrange("p (b t) -> p b t", b=STREAMS).unsqueeze(1).to_broadcast([P, 2, STREAMS, STEP])
                dve.tensor_tensor(u_s, xs, rs_s, ALU.mult).then_inc(xr_ready, 1)
                dve.wait_ge(xr_ready, 8 + j + 1)
                step.mark(dve.tensor_tensor(u_s, u_s, per_stream(coef[:, 2 * j:2 * j + 2, :], 2), ALU.mult))
                own()
                dve.tensor_tensor(u_s, u_s, per_stream(modT[:, 1, SHIFT1 + 2 * j:SHIFT1 + 2 * j + 2, :], 2), ALU.add).then_inc(hs_ready, 1)
                dve.wait_ge(hs_ready, 8 + j + 1)
                dve.wait_ge(hist_taken, j + 1)
                dve.wait_ge(u_ready, j + 1)
                src, span = ext, 1
                for dst in (sum_a, sum_b, sum_a, sum_b)[:g + 1]:
                    n0 = 2 * span - 1
                    step.mark(dve.tensor_tensor(dst[:, :, n0:EXT], src[:, :, n0:EXT], src[:, :, n0 - span:EXT - span], ALU.add))
                    own()
                    src, span = dst, 2 * span
                s_p, s_s, _ = ext_views(src)
                dif = sum_b if src is sum_a else sum_a
                d_p = dif[:, :, 0:PROMPT]
                d_s = dif[:, :, PROMPT:TOK].rearrange("p k (b t) -> p k b t", b=STREAMS)
                for k in range(2):
                    step.mark(dve.scalar_tensor_tensor(d_s[:, k], s_s[:, k], 1.0 / w, u_s[:, k], ALU.mult, ALU.subtract))
                step.mark(dve.scalar_tensor_tensor(d_p[:, :, 16:], s_p[:, :, 16:], 1.0 / w, u_p[:, :, 16:], ALU.mult, ALU.subtract))
                step.mark(dve.tensor_tensor(d_p[:, :, 0:16], s_p[:, :, 0:16], icount[:, g].unsqueeze(1).to_broadcast([P, 2, 16]), ALU.mult))
                own()
                dve.tensor_tensor(d_p[:, :, 0:16], d_p[:, :, 0:16], u_p[:, :, 0:16], ALU.subtract).then_inc(dif_ready, 1)
                dve.wait_ge(difhi_ready, j + 1)
                dve.tensor_tensor(h_lo[:, 2 * j:2 * j + 2, :], dif[:, :, 0:TOK], h_hi[:, 2 * j:2 * j + 2, :].bitcast(f32),
                                  ALU.subtract).then_inc(dif_split, 1)
                if j >= 3 and j % 2:
                    pooled(g - 1)
            pooled(3)
            dve.wait_ge(pool_stored, 16 * 9 * 8)
            norm_root(3)
            norm_apply(3)
            with loop(dve, 0, CHUNKS - 1, {step: 4 * ADD}) as c:
                ffn_chunk(W_FFN1 + c * 3, c + CHUNKS, 1, R_FFN1 + c * 4, False)
            ffn_chunk(W_FFN1 + 3 * (CHUNKS - 1), 2 * CHUNKS - 1, 1, R_FFN1 + 4 * (CHUNKS - 1), False, last=True)

            for i in range(0, 12, 2):
                t, q = i % TT, i // TT
                dve.wait_ge(yT_done, i + 1)
                dve.tensor_copy(yrow[:, t, q * 512:(q + 1) * 512], bank[:, i % 6]).then_inc(y_dve, 1)

        @block.tensor
        def _(pe):
            def product(out, w, wl, a, al, start, stop):
                pe.matmul(out, w, a, start=start, stop=False)
                pe.matmul(out, w, al, start=False, stop=False)
                return pe.matmul(out, wl, a, start=False, stop=stop)

            def ada_block(W, a, acc_bank, first=False):
                if not first:
                    pe.wait_ge(mod_ready, a)
                for s in range(4):
                    pe.wait_ge(lo_ready, 4 * W + s + 1)
                    for k in range(4):
                        kt = 4 * s + k
                        lhs = c18[:, kt * C18:kt * C18 + 66]
                        pe.matmul(bank[0:66, acc_bank, :], lhs, w_hi[:, s, k], start=(kt == 0), stop=False)
                        last = pe.matmul(bank[0:66, acc_bank, :], lhs, w_lo[:, s, k], start=False, stop=(kt == KT - 1))
                    last.then_inc(sub_used, 1)

            def ada_turn(a, t_bank, first=False):
                pe.wait_ge(mod_ready, a + 1)
                if not first:
                    pe.wait_ge(ada_done, a)
                for t in range(4):
                    last = pe.matmul(bank[:, t_bank, t * NC:(t + 1) * NC], mod18[:, t * P:(t + 1) * P], fold[:], start=True, stop=True)
                last.then_inc(ada_t, 1)

            def norm_stats(n):
                stat_bank = STAT_BANK[n]
                for g in range(4):
                    pe.wait_ge(sq_ready, 4 * n + g + 1)
                    for k in range(4):
                        last = pe.matmul(bank[:, stat_bank, 0:TOK], ones[:], nbuf[:, g % 2, k, :],
                                         start=(g + k == 0), stop=(g + k == 6))
                    last.then_inc(sq_used, 1)

            def to_features(W, s, b0, act_h, act_l, k0, start, stop):
                pe.wait_ge(lo_ready, 4 * W + s + 1)
                for k in range(4):
                    for m in range(4):
                        cols = slice(m * P, (m + 1) * P)
                        last = product(bank[:, b0 + m, 0:TOK], w_hi[:, s, k, cols], w_lo[:, s, k, cols],
                                       act_h[:, k0 + k, :], act_l[:, k0 + k, :], start and k == 0, stop and k == 3)
                last.then_inc(sub_used, 1)

            def to_tokens(W, b0):
                for s in range(4):
                    pe.wait_ge(lo_ready, 4 * W + s + 1)
                    pe.wait_ge(h_ready, s + 1)
                    for k in range(4):
                        kt = 4 * s + k
                        for t in range(TT):
                            cols = slice(t * P, (t + 1) * P)
                            out = bank[:, b0 + t, :]
                            pe.matmul(out, h_hi[:, kt, cols], w_hi[:, s, k], start=(kt == 0), stop=False)
                            pe.matmul(out, h_hi[:, kt, cols], w_lo[:, s, k], start=False, stop=False)
                            last = pe.matmul(out, h_lo[:, kt, cols], w_hi[:, s, k], start=False, stop=(kt == KT - 1))
                    last.then_inc(sub_used, 1)

            pe.wait_ge(const_ready, 1)
            pe.wait_ge(silu_c, 1)
            for k in range(KT):
                last = pe.transpose(bank[:, 6, k * NC:(k + 1) * NC], csil[:, k * P:(k + 1) * P], ident[0:NC, 0:NC])
            last.then_inc(cT_done, 1)
            pe.wait_ge(par_loaded, 16 * 7)
            for i, n in enumerate((96, 96, 80)):
                last = pe.transpose(bank[:, 7, i * 96:i * 96 + n], prow[0:n, i], ident[0:n, 0:n])
            last.then_inc(parT_done, 1)
            pe.wait_ge(x_loaded, 16 * TT)
            for i in range(12):
                t, q = i // 4, i % 4
                if i >= 6:
                    pe.wait_ge(xT_act if i % 2 else xT_dve, (i - 6) // 2 + 1)
                for k in range(4):
                    c = (4 * q + k) * P
                    last = pe.transpose(bank[:, i % 6, k * P:(k + 1) * P], xrow[:, t, c:c + P], ident[:])
                last.then_inc(xT_done, 1)

            pe.wait_ge(c18_ready, 3)
            ada_block(0, 0, 6, first=True)
            pe.wait_ge(par_ready, 1)
            ada_turn(0, 7, first=True)
            with pe.Fori(1, 8) as a:
                ada_block(a, a, 6)
                ada_turn(a, 7)
            pe.wait_ge(xT_dve, 6)
            pe.wait_ge(xT_act, 6)
            norm_stats(0)

            def qkv_group(g, first):
                W = W_QKV + 7 * g
                a = 8 + 4 * g
                if not first:
                    pe.wait_ge(v_taken, g)
                to_tokens(W, 0)
                ada_block(W + 1, a, 6)
                if not first:
                    pe.wait_ge(qk_taken, 2 * g)
                to_tokens(W + 2, 3)
                ada_turn(a, 7)
                ada_block(W + 3, a + 1, 6)
                pe.wait_ge(qk_taken, 2 * g + 1)
                to_tokens(W + 4, 0)
                ada_turn(a + 1, 7)
                ada_block(W + 5, a + 2, 6)
                ada_turn(a + 2, 7)
                ada_block(W + 6, a + 3, 6)
                ada_turn(a + 3, 7)

            qkv_group(0, True)
            with pe.Fori(1, HG) as g:
                qkv_group(g, False)

            with pe.Fori(0, HG) as g:
                pe.wait_ge(tok_loaded, 80 * g + 80)
                pe.wait_ge(banks_free, g + 1)
                for h in range(4):
                    for i in range(2):
                        for t in range(TT):
                            last = pe.transpose(bank[:, 4 * i + h, t * P:(t + 1) * P],
                                                tok[:, i, t, h * HD:(h + 1) * HD], ident[:])
                last.then_inc(qkT_done, 1)
                pe.wait_ge(qT_ready, g + 1)
                pe.wait_ge(kT_ready, g + 1)
                for h in range(4):
                    pe.matmul(bank[:, h, 0:256], kT[:, h, 0:P], qT[:, h, 0:256], start=True, stop=True)
                    pe.matmul(bank[:, h, 256:384], kT[:, h, P:2 * P], qT[:, h, P:2 * P], start=True, stop=True)
                    last = pe.matmul(bank[:, h, 384:512], kT[:, h, 2 * P:3 * P], qT[:, h, 2 * P:3 * P], start=True, stop=True)
                last.then_inc(zself_done, 1)

                def turn_keys(b):
                    pe.wait_ge(kv_loaded[b % 4], 64 * g + 16 * (b // 4) + 16)
                    if b:
                        pe.wait_ge(cT_act, 8 * g + b)
                        pe.wait_ge(cT_dve, 8 * g + b)
                    for h in range(4):
                        for k in range(PKT):
                            last = pe.transpose(bank[:, 4 + h, k * P:(k + 1) * P], raw[:, b % 4, k, h * HD:(h + 1) * HD], ident[:])
                    last.then_inc(kv_used, 1)

                def past_scores(b):
                    pe.wait_ge(cT_act, 8 * g + b + 1)
                    pe.wait_ge(cT_dve, 8 * g + b + 1)
                    if b >= 2:
                        pe.wait_ge(zpast_taken, 8 * g + b - 1)
                    else:
                        pe.wait_ge(zself_taken, g + 1)
                    q = PROMPT + b * STEP
                    for h in range(4):
                        for k in range(PKT):
                            c = (h * PKT + k) * STEP
                            last = pe.matmul(bank[:, b % 2, c:c + STEP], cacheT[:, b % 2, h, k * P:(k + 1) * P],
                                             qT[:, h, q:q + STEP], start=True, stop=True)
                    last.then_inc(zpast_done, 1)

                def self_sums(p):
                    pe.wait_ge(sp_ready, 4 * g + p + 1)
                    if p:
                        pe.wait_ge(oself_taken, 2 * g + 1)
                    else:
                        pe.wait_ge(zself_taken, g + 1)
                    for i in range(2):
                        pe.matmul(bank[:, 2 + i, :], tri[:], sp_buf[:, i, :], start=True, stop=False)
                        last = pe.matmul(bank[:, 2 + i, P:2 * P], ones[:], sp_buf[:, i, 256:384], start=False, stop=True)
                    last.then_inc(tri_done, 1)

                def self_values(p):
                    pe.wait_ge(w_ready, 4 * g + p + 1)
                    for i in range(2):
                        h = 2 * p + i
                        v = [tok[:, 2, t, h * HD:(h + 1) * HD] for t in range(TT)]
                        b = bank[:, 2 + i]
                        pe.matmul(b[:, 256:384], v[2], zs_self[:, h, 384:512], start=True, stop=True)
                        pe.matmul(b[:, 0:256], v[0], zs_self[:, h, 0:256], start=True, stop=False)
                        last = pe.matmul(b[:, P:256], v[1], zs_self[:, h, 256:384], start=False, stop=True)
                    last.then_inc(oself_done, 1)

                turn_keys(0)
                turn_keys(1); past_scores(0)
                turn_keys(2); past_scores(1)
                turn_keys(3); past_scores(2)
                self_sums(0)
                turn_keys(4); past_scores(3)
                self_values(0)
                turn_keys(5); past_scores(4)
                turn_keys(6); past_scores(5)
                self_sums(1)
                turn_keys(7); past_scores(6)
                past_scores(7)
                self_values(1)
                for p in range(2):
                    pe.wait_ge(later_ready, 2 * g + p + 1)
                    if p:
                        pe.wait_ge(t_ready, 4 * g + 3)
                    else:
                        pe.wait_ge(oself_taken, 2 * g + 2)
                    for i in range(2):
                        pe.matmul(bank[:, 2 + i, :], tri[:], sp_buf[:, i, :], start=True, stop=False)
                        last = pe.matmul(bank[:, 2 + i, :], ones[:], later[:, 2 * p + i].rearrange("p k t -> p (k t)"),
                                         start=False, stop=True)
                    last.then_inc(tri_done, 1)
                pe.wait_ge(w_ready, 4 * g + 4)
                for b in range(STREAMS):
                    pe.wait_ge(kv_loaded[b % 4], 64 * g + 32 + 16 * (b // 4) + 16)
                    for h in range(4):
                        for k in range(PKT):
                            c = h * SAMPLE + b * STEP
                            last = pe.matmul(bank[:, 4, c:c + STEP], raw[:, b % 4, k, h * HD:(h + 1) * HD],
                                             zs_past[:, h, k, b, :], start=(k == 0), stop=(k == PKT - 1))
                    last.then_inc(kv_used, 1)

            pe.wait_ge(banks_free, HG + 1)
            for i in range(2):
                W = W_O + 3 * i
                for b in range(2):
                    if i:
                        pe.wait_ge(residual_taken, 2 * i + b - 1)
                        if b == 0:
                            pe.wait_ge(mod_ready, 25)
                            pe.wait_ge(ada_done, 25)
                    for s in range(4):
                        to_features(W + b, s, 4 * b, h_hi, h_lo, 4 * s, s == 0, s == 3)
                pe.wait_ge(residual_taken, 2 * i + 1)
                ada_block(W + 2, 24 + i, 0)
                ada_turn(24 + i, 1)
            pe.wait_ge(residual_taken, 3)
            norm_stats(1)

            def ffn_chunk(W, c, r, hr, with_ada):
                pe.wait_ge(residual_taken, r if with_ada else r - 1)
                for s in range(4):
                    pe.wait_ge(h_ready, hr + s + 1)
                    to_features(W, s, 0, h_hi, h_lo, 4 * s, s == 0, s == 3)
                if not with_ada:
                    pe.wait_ge(residual_taken, r)
                for s in range(4):
                    to_features(W + 1, s, 4, h_hi, h_lo, 4 * s, s == 0, s == 3)
                down = W + 2
                if with_ada:
                    a = 26 + 2 * c
                    pe.wait_ge(gate_taken, c + 1)
                    ada_block(W + 2, a, 0)
                    ada_block(W + 3, a + 1, 1, first=True)
                    ada_turn(a, 2)
                    down = W + 4
                for s in range(4):
                    if s == 0:
                        pe.wait_ge(lo_ready, 4 * down + 1)
                        for k in range(4):
                            if k == 0 and with_ada:
                                pe.wait_ge(act_ready, 4 * c + 4)
                            elif not with_ada:
                                pe.wait_ge(act_ready, 4 * c + k + 1)
                            for m in range(4):
                                cols = slice(m * P, (m + 1) * P)
                                last = product(bank[:, down_bank(0, with_ada) + m, 0:TOK], w_hi[:, 0, k, cols], w_lo[:, 0, k, cols],
                                               act_hi[:, k, :], act_lo[:, k, :], k == 0, k == 3)
                        last.then_inc(sub_used, 1)
                        if with_ada:
                            ada_turn(a + 1, 3)
                    else:
                        if s == 1:
                            if with_ada:
                                pe.wait_ge(ada_done, a + 2)
                            else:
                                pe.wait_ge(act_ready, 4 * c + 4)
                        if s >= 2:
                            pe.wait_ge(residual_taken, r + s - 1)
                        to_features(down, s, down_bank(s, with_ada), act_hi, act_lo, 0, True, True)

            with pe.Fori(0, CHUNKS) as c:
                ffn_chunk(W_FFN0 + c * 5, c, R_FFN0 + c * 4, 4, True)

            pe.wait_ge(residual_taken, R_POOL)
            norm_stats(2)
            u_p, u_s, _ = ext_views(ext)
            for j in range(8):
                pe.wait_ge(hist_loaded[j % 2], 16 * (j // 2 + 1))
                if j:
                    pe.wait_ge(hist_taken, j)
                for k in range(2):
                    last = pe.transpose(bank[:, 1, 120 * k:120 * (k + 1)], hrow[:, j % 2, k * P:(k + 1) * P], ident[0:120, 0:120])
                last.then_inc(hist_done, 1)
                pe.wait_ge(u_ready, j + 1)
                if j:
                    pe.wait_ge(uT_taken, j)
                for k in range(2):
                    pe.transpose(bank[:, 0, k * P:(k + 1) * P], ext[:, k, STATE + P:STATE + PROMPT], ident[:])
                    last = pe.transpose(bank[:, 0, 256 + k * P:256 + (k + 1) * P], u_dense[:, k], ident[:])
                last.then_inc(uT_done, 1)
                if j % 2:
                    s = j // 2
                    pe.wait_ge(dif_split, j + 1)
                    if s:
                        pe.wait_ge(residual_taken, R_POOL + s)
                    to_features(W_POOL, s, 4, h_hi, h_lo, 4 * s, True, True)
            pe.wait_ge(residual_taken, R_FFN1)
            norm_stats(3)
            with pe.Fori(0, CHUNKS) as c:
                ffn_chunk(W_FFN1 + c * 3, c + CHUNKS, R_FFN1 + c * 4, 8, False)

            for i in range(12):
                t, q = i % TT, i // TT
                if i == 0:
                    pe.wait_ge(residual_taken, R_END)
                if i >= 6:
                    pe.wait_ge(y_act if i % 2 else y_dve, (i - 6) // 2 + 1)
                for k in range(4):
                    last = pe.transpose(bank[:, i % 6, k * P:(k + 1) * P], x[:, 4 * q + k, t * P:(t + 1) * P], ident[:])
                last.then_inc(yT_done, 1)


INPUTS = ["x_prompt", "x_sample", "c_prompt", "c_sample", "cache_k", "cache_v", "state_pool", "w_ada",
          "b_ada", "g_mix", "g_ffn", "w_qkv", "g_q", "g_k", "w_o", "w_pool", "pool_scale", "w_gate",
          "w_up", "w_down"]
OUTPUTS = [(1, PROMPT, D), (STREAMS, STEP, D), (1, 1, PROMPT, NH, HD), (1, 1, PROMPT, NH, HD),
           (1, 1, STATE, D), (1, STREAMS, STEP, NH, HD), (1, STREAMS, STEP, NH, HD),
           (1, STREAMS, STATE, D)]


def kernel(**inputs):
    import concourse.bacc as bacc
    from concourse.bass_utils import run_bass_kernel_spmd

    nc = bacc.Bacc("TRN2", target_bir_lowering=False, num_devices=1)
    arrays, args = {}, []
    for name in INPUTS:
        a = np.ascontiguousarray(inputs[name])
        arrays[f"in_{name}"] = a
        args.append(nc.dram_tensor(f"in_{name}", a.shape, mybir.dt.from_np(a.dtype), kind="ExternalInput").ap())
    for i, shape in enumerate(OUTPUTS):
        args.append(nc.dram_tensor(f"out_{i}", shape, f32, kind="ExternalOutput").ap())
    encoder_step(nc, *args)
    got = run_bass_kernel_spmd(nc, [arrays], core_ids=[0]).results[0]
    return tuple(got[f"out_{i}"] for i in range(len(OUTPUTS)))
```

```python
from contextlib import ExitStack, contextmanager

import numpy as np
import concourse.bass as bass
from concourse import mybir

f32 = mybir.dt.float32
f32r = mybir.dt.float32r
ACT = mybir.ActivationFunctionType
ALU = mybir.AluOpType
AX = mybir.AxisListType
ds = bass.ds

P = 128
D = 2048
KT = D // P
NH, HD = 16, 128
PROMPT, STREAMS, STEP = 256, 8, 16
SAMPLE = STREAMS * STEP
TOK = PROMPT + SAMPLE
TT = TOK // P
PAST = 512
PKT = PAST // P
FF = 5632
CHUNKS = FF // 512
NC = 1 + STREAMS
NMOD = 6
MODT = NMOD * D // P
STATE = 15
WINDOWS = (2, 4, 8, 16)
EPS = 1e-6
SCALE = HD ** -0.5
HG = 4
HQ = 4 * STEP
WIN = P + STEP

W_ADA = 0
W_QKV = 8
W_O = W_QKV + 6 * HG
W_FFN0 = W_O + 10
W_POOL = W_FFN0 + 5 * CHUNKS
W_FFN1 = W_POOL + 1
W_END = W_FFN1 + 3 * CHUNKS
ADA_O, ADA_FFN = 8 + 3 * HG, 8 + 3 * HG + 6
R_O, R_FFN0, R_POOL = 0, 4, 4 + 4 * CHUNKS
R_FFN1 = R_POOL + 4
R_END = R_FFN1 + 4 * CHUNKS
SHIFT1, SCALE1, GATE1, SHIFT2, SCALE2, GATE2 = (i * KT for i in range(NMOD))
EXT = STATE + PROMPT + STREAMS * (STATE + STEP)
C18 = 2 * NC


class Tally:

    def __init__(self, sem):
        self.sem, self.base, self.n, self.i = sem, 0, 0, None

    def mark(self, instruction):
        instruction.then_inc(self.sem, 1)
        self.n += 1

    def value(self):
        v = self.base + self.n
        if self.i is not None:
            v = (self.i - self.lo) * self.per + v
        return v


@contextmanager
def loop(engine, lo, hi, per):
    with engine.Fori(lo, hi) as i:
        for t, k in per.items():
            t.base, t.n, t.i, t.lo, t.per = t.base + t.n, 0, i, lo, k
        yield i
        for t, k in per.items():
            assert t.n == k, (t.n, k)
            t.base, t.n, t.i = t.base + k * (hi - lo), 0, None


def encoder_step(nc, x_prompt, x_sample, c_prompt, c_sample, cache_k, cache_v, state_pool,
                 w_ada, b_ada, g_mix, g_ffn, w_qkv, g_q, g_k, w_o, w_pool, pool_scale,
                 w_gate, w_up, w_down,
                 y_prompt, y_sample, k_prompt, v_prompt, pool_prompt, k_sample, v_sample,
                 pool_sample):
    ctx = ExitStack()
    with ctx:
        sem_of = {}

        def sem(name):
            sem_of[name] = ctx.enter_context(nc.semaphore(name))
            return sem_of[name]

        q_scratch = nc.dram_tensor("q_scratch", (TOK, D), f32).ap()

        arena_start = (nc.sbuf_base + 31) // 32 * 32
        place = [0]

        def at(offset, name, shape, dt=f32):
            return nc.alloc_sbuf_tensor_at(name, shape, dt, offset=arena_start + offset)

        def nxt(name, shape, dt=f32):
            o = place[0]
            place[0] = (o + int(np.prod(shape[1:])) * 4 + 31) // 32 * 32
            return at(o, name, shape, dt), o

        x, _ = nxt("x", [P, KT, TOK])
        h_hi, H0 = nxt("h_hi", [P, KT, TOK], f32r)
        h_lo, _ = nxt("h_lo", [P, KT, TOK], f32r)
        raw, RAW = nxt("raw", [P, 4, 4, 512])
        w_hi, R1 = nxt("w_hi", [P, 4, 4, 512], f32r)
        w_lo, _ = nxt("w_lo", [P, 4, 4, 512], f32r)
        act_f, R2 = nxt("act_f", [P, 4, TOK])
        act_hi, _ = nxt("act_hi", [P, 4, TOK], f32r)
        act_lo, _ = nxt("act_lo", [P, 4, TOK], f32r)
        modT, _ = nxt("modT", [P, 2, MODT, NC])
        par, _ = nxt("par", [P, 2 * MODT + 5 * KT])
        coef, _ = nxt("coef", [P, KT, NC])
        c18, _ = nxt("c18", [P, KT * C18 + 48], f32r)
        ident, _ = nxt("ident", [P, P])
        ones, _ = nxt("ones", [P, P])
        tri, _ = nxt("tri", [P, P])
        mask, _ = nxt("mask", [P, 512])
        fold, _ = nxt("fold", [C18, NC])
        mod18, _ = nxt("mod18", [C18, 512])
        gqk, _ = nxt("gqk", [P, 2, HD])
        rsb, _ = nxt("rsb", [P, TOK])
        qk_rs, _ = nxt("qk_rs", [P, 2, 12])
        exponent, _ = nxt("exponent", [P, 8])
        tmp_s, _ = nxt("tmp_s", [P, 4, SAMPLE])
        icount, _ = nxt("icount", [P, 4, 16])
        xrow = at(H0, "xrow", [P, TT, D])
        crow = at(H0 + 24576, "crow", [NC, D])
        csil = at(H0 + 32768, "csil", [NC, D])
        prow = at(H0 + 40960, "prow", [96, 3, P])
        yrow = at(H0, "yrow", [P, TT, D])
        nbuf = at(R2, "nbuf", [P, 2, 4, TOK])
        sq_sum = at(R2 + 12288, "sq_sum", [P, 4, TOK])
        sq = at(R2, "sq", [P, TT, 512])
        qkv_out = at(R2 + 6144, "qkv_out", [P, 2, TT, 512])
        ext = at(R2, "ext", [P, 2, EXT])
        sum_a = at(R2 + 4160, "sum_a", [P, 2, EXT])
        sum_b = at(R2 + 8320, "sum_b", [P, 2, EXT])
        urow = at(R2 + 12480, "urow", [P, 2, 256])
        hrow = at(R2 + 14528, "hrow", [STREAMS * STATE, 2, 256])
        u_dense = at(R2 + 16576, "u_dense", [P, 2, SAMPLE])
        zs_self = at(R2, "zs_self", [P, 4, 512])
        e_buf = at(R2 + 8192, "e_buf", [P, 2, 512])
        sp_buf = at(R2 + 12288, "sp_buf", [P, 2, 512])
        o_new = at(R2 + 16384, "o_new", [P, 4, SAMPLE])
        tok = at(R1, "tok", [P, 3, TT, 512])
        qT = at(R1 + 18432, "qT", [P, 4, TOK])
        kT = at(R1 + 24576, "kT", [P, 4, TOK])
        zs_past = at(R1 + 30720, "zs_past", [P, STREAMS, PKT, HQ])
        later = at(R1 + 38912, "later", [P, STREAMS, PKT, HQ])
        s_hi = at(R1 + 47104, "s_hi", [P, 2, 4, 512], f32r)
        s_lo = at(RAW, "s_lo", [P, 4, 4, 512], f32r)
        q_win = at(R1, "q_win", [P, 2, 4 * WIN], f32r)
        z_row = at(R1 + 4608, "z_row", [P, 2, 512])
        o_row = at(R1 + 18432, "o_row", [P, 2, 512])
        w_st = at(R1 + 24576, "w_st", [P, 2, PKT, P], f32r)
        o_f = at(R1 + 63488, "o_f", [P, 4, SAMPLE])

        bank = ctx.enter_context(nc.psum_tensor("bank", [P, 8, 512], f32))

        raw_loaded = [sem(f"raw_loaded{s}") for s in range(4)]
        hi_ready, lo_ready, sub_used = sem("hi_ready"), sem("lo_ready"), sem("sub_used")
        pool_step, const_ready = sem("pool_step"), sem("const_ready")
        x_loaded, c_loaded, par_loaded = sem("x_loaded"), sem("c_loaded"), sem("par_loaded")
        gqk_loaded, silu_c = sem("gqk_loaded"), sem("silu_c")
        xT_done, xT_dve, xT_act = sem("xT_done"), sem("xT_dve"), sem("xT_act")
        cT_done, c18_ready, parT_done, par_ready = sem("cT_done"), sem("c18_ready"), sem("parT_done"), sem("par_ready")
        mod_ready, ada_t, ada_done = sem("mod_ready"), sem("ada_t"), sem("ada_done")
        sq_ready, quad_summed, sq_used = sem("sq_ready"), sem("quad_summed"), sem("sq_used")
        var_ready, std_ready = sem("var_ready"), sem("std_ready")
        xr_ready, hs_ready, hhi_ready, h_ready = sem("xr_ready"), sem("hs_ready"), sem("hhi_ready"), sem("h_ready")
        dve_step, act_step = sem("dve_step"), sem("act_step")
        qksq_ready, qkvar_ready, qkrs_ready = sem("qksq_ready"), sem("qkvar_ready"), sem("qkrs_ready")
        qk_taken, qk_ready, v_taken = sem("qk_taken"), sem("qk_ready"), sem("v_taken")
        stored = [sem("stored_qv"), sem("stored_k")]
        kv_loaded = [sem(f"kv_loaded{s}") for s in range(4)]
        kv_used, tok_loaded = sem("kv_used"), sem("tok_loaded")
        group_done, kturn_done, qkT_done, qT_ready, kT_ready = sem("group_done"), sem("kturn_done"), sem("qkT_done"), sem("qT_ready"), sem("kT_ready")
        zself_done, zself_taken = sem("zself_done"), sem("zself_taken")
        win_clear, qhi_ready, q_split = sem("win_clear"), sem("qhi_ready"), sem("q_split")
        turned, cache_hi, cache_lo = sem("turned"), sem("cache_hi"), sem("cache_lo")
        zrow_ready, zpast_done, zpast_taken = sem("zrow_ready"), sem("zpast_done"), sem("zpast_taken")
        whi_ready, w_split, half_used = sem("whi_ready"), sem("w_split"), sem("half_used")
        orow_ready, opast_done, opast_taken = sem("orow_ready"), sem("opast_done"), sem("opast_taken")
        ln_ready, sp_ready, tri_done, t_ready = sem("ln_ready"), sem("sp_ready"), sem("tri_done"), sem("t_ready")
        w_ready, oself_done, ohi_ready, oself_taken = sem("w_ready"), sem("oself_done"), sem("ohi_ready"), sem("oself_taken")
        later_ready, ofhi_ready, o_split = sem("later_ready"), sem("ofhi_ready"), sem("o_split")
        gate_taken, up_tile, act_f_ready, act_hi_ready, act_ready = sem("gate_taken"), sem("up_tile"), sem("act_f_ready"), sem("act_hi_ready"), sem("act_ready")
        residual_taken = sem("residual_taken")
        hist_loaded = [sem("hist_loaded0"), sem("hist_loaded1")]
        hist_done, hist_taken = sem("hist_done"), sem("hist_taken")
        u_ready, uT_done, uT_taken, pool_stored = sem("u_ready"), sem("uT_done"), sem("uT_taken"), sem("pool_stored")
        dif_ready, difhi_ready, dif_split = sem("dif_ready"), sem("difhi_ready"), sem("dif_split")
        yT_done, y_dve, y_act, y_stored = sem("yT_done"), sem("y_dve"), sem("y_act"), sem("y_stored")

        def rows(w):
            return w.rearrange("(k p) n -> p k n", p=P)

        def ada_src(layer, j, s):
            return rows(w_ada[layer, s * 512:(s + 1) * 512, ds(j * 512, 512)])

        def quads(t, k0, n=4):
            v = t[:, k0:k0 + n, :]
            return v[:, :, 0:PROMPT], v[:, :, PROMPT:TOK].rearrange("p k (b t) -> p k b t", b=STREAMS)

        def per_stream(m, n=4):
            return m[:, :, 1:NC].unsqueeze(3).to_broadcast([P, n, STREAMS, STEP])

        def ext_views(t, n=2):
            s = t[:, 0:n, STATE + PROMPT:EXT].rearrange("p k (b t) -> p k b t", b=STREAMS)
            return t[:, 0:n, STATE:STATE + PROMPT], s[:, :, :, STATE:STATE + STEP], s[:, :, :, 0:STATE]

        def half(t, q):
            return t[:, 4 * q:4 * q + 4].rearrange("p (i b) k n -> p i (b k n)", i=2)

        parG = par[:, 2 * MODT:]
        c_hi = c18[:, 0:KT * C18].rearrange("p (k c) -> p k c", c=C18)
        hist_rows = state_pool[0].rearrange("b t n -> (b t) n")

        def norm_plan(n):
            layer, ffn = n // 2, n % 2
            return (SCALE2 if ffn else SCALE1), (SHIFT2 if ffn else SHIFT1), KT * (2 * ffn + layer), layer

        def down_bank(s, with_ada):
            return 4 if (s % 2 == 0) == with_ada else 0

        def acc_bank(i):
            return 4 * (1 - i % 2)

        BETWEEN_0 = [[(W_QKV + 1, g)] for g in range(4)]
        BETWEEN_1 = [[(W_FFN0, 0), (W_FFN0, 1)], [(W_FFN0, 2), (W_FFN0, 3)], [(W_FFN0 + 1, 0)], [(W_FFN0 + 1, 1)]]
        BETWEEN_3 = [[(W_FFN1, g)] for g in range(4)]

        XR, HR = (0, 4, 8, 16), (0, 4, 8, 8)
        STAT_BANK = (5, 2, 4, 4)

        block = ctx.enter_context(nc.Block())

        @block.sync
        def _(sp):
            def load(W, s, src, first=False):
                if not first:
                    sp.wait_ge(lo_ready, 4 * W + s - 3)
                sp.dma_start(raw[:, s], src).then_inc(raw_loaded[s], 16)

            def load_ada(W, layer, j, first=False):
                for s in range(4):
                    load(W, s, ada_src(layer, j, s), first)

            def load_cols(W, w, col):
                for s in range(4):
                    load(W, s, rows(w[s * 512:(s + 1) * 512, ds(col, 512)]))

            load_ada(0, 0, 0, first=True)
            with sp.Fori(1, 8) as j:
                load_ada(j, 0, j)
            with sp.Fori(0, HG) as g:
                W = W_QKV + g * 6
                for i in range(3):
                    load_ada(W + 2 * i, 0, g * 3 + (8 + i))
                    load_cols(W + 2 * i + 1, w_qkv[0], g * 512 + i * D)

            def load_cache(col, j, ahead=0):
                src = (cache_k if j < 8 else cache_v)[0, j % 8].rearrange("(k p) h d -> p k (h d)", p=P)
                sp.dma_start(raw[:, j % 4], src[:, :, ahead:][:, :, ds(col, 512)]).then_inc(kv_loaded[j % 4], 16)

            def load_tok(col, ahead=0):
                cols = ds(col, 512)
                flat = "b t h d -> (b t) (h d)"
                sp.dma_start(tok[:, 0], q_scratch[:, ahead:][:, cols].rearrange("(t p) n -> p t n", p=P)).then_inc(tok_loaded, 16)
                for i, (a, b) in ((1, (k_prompt, k_sample)), (2, (v_prompt, v_sample))):
                    sp.dma_start(tok[:, i, 0:2], a[0].rearrange(flat)[:, ahead:][:, cols].rearrange("(t p) n -> p t n", p=P)).then_inc(tok_loaded, 16)
                    sp.dma_start(tok[:, i, 2], b[0].rearrange(flat)[:, ahead:][:, cols]).then_inc(tok_loaded, 16)

            def cache_rest(g, col):
                for j in range(4, 16):
                    if j != 8:
                        sp.wait_ge(kv_used, 16 * g + (5 if j == 7 else j - 3))
                    load_cache(col, j)

            for s in range(4):
                sp.wait_ge(lo_ready, 4 * (W_O - 1) + s + 1)
                load_cache(0, s)
            sp.wait_ge(sub_used, 4 * W_O)
            sp.wait_ge(stored[0], 16 * 4 * (HG - 1))
            sp.wait_ge(stored[1], 16 * 2 * (HG - 1))
            load_tok(0)
            with sp.Fori(0, HG - 1) as g:
                col = sp.snap(g * 512)
                cache_rest(g, col)
                sp.wait_ge(oself_done, 2 * g + 2)
                sp.wait_ge(stored[0], 16 * 4 * HG)
                sp.wait_ge(stored[1], 16 * 2 * HG)
                load_tok(col, 512)
                for j in range(4):
                    sp.wait_ge(kv_used, 16 * g + 13 + j)
                    load_cache(col, j, 512)
            cache_rest(HG - 1, 512 * (HG - 1))

            for i in range(6):
                if i < 4:
                    for s in range(4):
                        src = rows(w_o[0, s * 512:(s + 1) * 512, i * 512:(i + 1) * 512])
                        if i == 0:
                            sp.wait_ge(kv_used, 16 * HG - 3 + s)
                            sp.dma_start(raw[:, s], src).then_inc(raw_loaded[s], 16)
                        else:
                            load(W_O + 2 * i, s, src)
                a = ADA_O + i
                load_ada(W_O + (2 * i + 1 if i < 4 else 4 + i), a // 24, a % 24)

            def load_down(W, layer, c):
                for s in range(4):
                    load(W, s, rows(w_down[layer, ds(c * 512, 512), s * 512:(s + 1) * 512]))

            with sp.Fori(0, CHUNKS) as c:
                W = W_FFN0 + c * 5
                load_ada(W, 1, c * 2 + (ADA_FFN - 24))
                load_cols(W + 1, w_gate[0], c * 512)
                load_cols(W + 2, w_up[0], c * 512)
                load_ada(W + 3, 1, c * 2 + (ADA_FFN - 23))
                load_down(W + 4, 0, c)
            for s in range(4):
                load(W_POOL, s, rows(w_pool[0, s]))
            load_cols(W_FFN1, w_gate[1], 0)
            for j in range(8):
                sp.wait_ge(uT_taken, j + 1)
                cols = slice(256 * j, 256 * j + 256)
                sp.dma_start(pool_prompt[0, 0, :, cols], urow[P - STATE:P, 0, :]).then_inc(pool_stored, 16)
                for b in range(STREAMS):
                    sp.dma_start(pool_sample[0, b, :, cols],
                                 urow[STEP * b + 1:STEP * (b + 1), 1, :]).then_inc(pool_stored, 16)
            load_cols(W_FFN1 + 1, w_up[1], 0)
            load_down(W_FFN1 + 2, 1, 0)
            with sp.Fori(1, CHUNKS) as c:
                W = W_FFN1 + c * 3
                load_cols(W, w_gate[1], c * 512)
                load_cols(W + 1, w_up[1], c * 512)
                load_down(W + 2, 1, c)
            sp.wait_ge(pool_stored, 16 * 9 * 8)
            sp.wait_ge(y_act, 6)
            sp.wait_ge(y_dve, 6)
            for t in range(TT):
                dst = y_prompt[0, t * P:(t + 1) * P] if t < 2 else y_sample.rearrange("b t n -> (b t) n")
                sp.dma_start(dst, yrow[:, t]).then_inc(y_stored, 16)
            sp.wait_ge(y_stored, 16 * TT)

        @block.gpsimd
        def _(pool):
            step = Tally(pool_step)

            def do(ins):
                step.mark(ins)
                pool.wait_ge(pool_step, step.value())

            do(pool.memset(ident[:], 0.0))
            do(pool.affine_select(out=ident[:], in_=ident[:], compare_op=ALU.not_equal, fill=1.0, base=0,
                                  pattern=[[-1, P]], channel_multiplier=1))
            do(pool.memset(ones[:], 1.0))
            do(pool.memset(exponent[:], -0.5))
            do(pool.affine_select(out=tri[:], in_=ones[:], compare_op=ALU.is_ge, fill=0.0, base=0,
                                  pattern=[[-1, P]], channel_multiplier=1))
            do(pool.memset(mask[:], 3e38))
            for c0, n in ((0, 256), (256, 128), (384, 128)):
                part = mask[:, c0:c0 + n]
                do(pool.affine_select(out=part, in_=part, compare_op=ALU.is_gt, fill=-1e30, base=0,
                                      pattern=[[1, n]], channel_multiplier=-1))
            part = mask[:, 384:512].rearrange("p (b t) -> p b t", b=STREAMS)
            do(pool.affine_select(out=part, in_=part, compare_op=ALU.is_ge, fill=-1e30, base=0,
                                  pattern=[[-STEP, STREAMS], [0, STEP]], channel_multiplier=1))
            do(pool.memset(fold[:], 0.0))
            for off in (0, NC):
                do(pool.affine_select(out=fold[:], in_=fold[:], compare_op=ALU.not_equal, fill=1.0, base=-off,
                                      pattern=[[-1, NC]], channel_multiplier=1))
            for i in range(4):
                do(pool.iota(icount[:, i, :], pattern=[[1, 16]], base=1, channel_multiplier=0,
                             allow_small_or_imprecise_dtypes=True))
            pool.memset(tmp_s[:, 0, 0:1], 0.0).then_inc(const_ready, 1)

            with pool.Fori(0, HG) as g:
                for i in range(2):
                    pool.wait_ge(qkvar_ready, 2 * g + i + 1)
                    r = qk_rs[:, i]
                    pool.tensor_tensor(r, r, exponent[:, 0:1].to_broadcast([P, 12]), ALU.pow).then_inc(qkrs_ready, 1)
            with pool.Fori(0, HG) as g:
                for b in range(STREAMS):
                    pool.wait_ge(whi_ready, 8 * g + b + 1)
                    pool.tensor_tensor(w_st[:, b % 2, :, HQ:P], zs_past[:, b], w_st[:, b % 2, :, 0:HQ].bitcast(f32),
                                       ALU.subtract).then_inc(w_split, 1)

            def split_acts(lo, hi):
                with pool.Fori(lo, hi) as c:
                    for m in range(4):
                        pool.wait_ge(act_hi_ready, 4 * c + m + 1)
                        pool.tensor_tensor(act_lo[:, m], act_f[:, m], act_hi[:, m].bitcast(f32), ALU.subtract).then_inc(act_ready, 1)

            split_acts(0, CHUNKS)
            for j in range(8):
                dif = (sum_b, sum_a, sum_b, sum_a)[j // 2]
                pool.wait_ge(difhi_ready, j + 1)
                pool.tensor_tensor(h_lo[:, 2 * j:2 * j + 2, :], dif[:, :, 0:TOK], h_hi[:, 2 * j:2 * j + 2, :].bitcast(f32),
                                   ALU.subtract).then_inc(dif_split, 1)
            split_acts(CHUNKS, 2 * CHUNKS)

        @block.scalar
        def _(act):
            step = Tally(act_step)

            def hi(W, subs, first=False):
                for s in subs:
                    act.wait_ge(raw_loaded[s], 16 * W + 16)
                    if not first:
                        act.wait_ge(sub_used, 4 * W + s - 3)
                    act.activation(w_hi[:, s], raw[:, s], ACT.Copy).then_inc(hi_ready, 1)

            def mod_out(W, a, acc_bank, first=False):
                act.wait_ge(sub_used, 4 * W + 4)
                if not first:
                    act.wait_ge(ada_t, a)
                act.activation(mod18[:], bank[0:C18, acc_bank, :], ACT.Copy).then_inc(mod_ready, 1)

            def norm_stats(n):
                for g in range(4):
                    if n == 0:
                        act.wait_ge(xT_dve, 6)
                        act.wait_ge(xT_act, 6)
                    else:
                        act.wait_ge(residual_taken, (R_FFN0, R_POOL, R_FFN1)[n - 1] - 3 + g)
                    if n >= 2:
                        act.wait_ge(sub_used, 4 * (W_POOL, W_FFN1)[n - 2])
                    if g >= 2:
                        act.wait_ge(quad_summed, 4 * n + g - 1)
                    act.activation(nbuf[:, g % 2], x[:, 4 * g:4 * g + 4, :], ACT.Square).then_inc(sq_ready, 1)
                act.wait_ge(var_ready, n + 1)
                act.activation(rsb[:], rsb[:], ACT.Sqrt).then_inc(std_ready, 1)

            def norm_apply(n, between=((), (), (), ())):
                _, shift, _, layer = norm_plan(n)
                for g in range(4):
                    for W, s in between[g]:
                        hi(W, [s])
                    act.wait_ge(xr_ready, XR[n] + g + 1)
                    for k in range(4):
                        v = nbuf[:, g % 2, k, 0:PROMPT]
                        m = 4 * g + k
                        step.mark(act.activation(v, v, ACT.Identity, bias=modT[:, layer, shift + m, 0:1],
                                                 scale=coef[:, m, 0:1]))
                    act.wait_ge(act_step, step.value())
                    act.wait_ge(hs_ready, XR[n] + g + 1)
                    act.activation(h_hi[:, 4 * g:4 * g + 4, :], nbuf[:, g % 2], ACT.Copy).then_inc(hhi_ready, 1)

            act.dma_start(crow[0:1], c_prompt).then_inc(c_loaded, 16)
            act.dma_start(crow[1:NC], c_sample).then_inc(c_loaded, 16)
            for t in range(TT):
                src = x_prompt[0, t * P:(t + 1) * P] if t < 2 else x_sample.rearrange("b t n -> (b t) n")
                act.dma_start(xrow[:, t], src).then_inc(x_loaded, 16)
            for i in range(2):
                act.dma_start(prow[:, i], b_ada[i].rearrange("(a n) -> a n", n=P)).then_inc(par_loaded, 16)
            for i, g in enumerate((g_mix, g_ffn)):
                for l in range(2):
                    r = KT * (2 * i + l)
                    act.dma_start(prow[r:r + KT, 2], g[l].rearrange("(a n) -> a n", n=P)).then_inc(par_loaded, 16)
            act.dma_start(prow[4 * KT:5 * KT, 2], pool_scale[0].rearrange("(a n) -> a n", n=P)).then_inc(par_loaded, 16)
            for i, g in enumerate((g_q, g_k)):
                act.dma_start(gqk[:, i], g[0:1, :].to_broadcast([P, HD])).then_inc(gqk_loaded, 16)

            act.wait_ge(c_loaded, 32)
            act.activation(csil[:], crow[:], ACT.Silu).then_inc(silu_c, 1)
            hi(0, range(4), first=True)
            hi(1, range(3))
            mod_out(0, 0, 6, first=True)
            hi(1, [3])
            for i in range(1, 12, 2):
                t, q = i // 4, i % 4
                act.wait_ge(xT_done, i + 1)
                act.activation(x[:, 4 * q:4 * q + 4, t * P:(t + 1) * P],
                               bank[:, i % 6].rearrange("p (k c) -> p k c", k=4), ACT.Copy).then_inc(xT_act, 1)
            norm_stats(0)
            with act.Fori(1, 8) as a:
                hi(a + 1, range(3))
                mod_out(a, a, 6)
                hi(a + 1, [3])
            norm_apply(0, BETWEEN_0)

            def square_heads(g, i):
                W = W_QKV + 6 * g + 2 * i + 1
                act.wait_ge(sub_used, 4 * W + 4)
                b0 = 3 * i
                if i:
                    act.wait_ge(qkvar_ready, 2 * g + i)
                act.activation(sq[:], bank[:, b0:b0 + 3, :], ACT.Square).then_inc(qksq_ready, 1)

            def store(g, i):
                flat = "b t h d -> (b t) (h d)"
                cols = ds(g * 512, 512)
                slot = (0, 1, 0)[i]
                a, b = ((q_scratch[0:PROMPT], q_scratch[PROMPT:TOK]),
                        (k_prompt[0].rearrange(flat), k_sample[0].rearrange(flat)),
                        (v_prompt[0].rearrange(flat), v_sample[0].rearrange(flat)))[i]
                if i < 2:
                    act.wait_ge(qk_ready, 2 * g + i + 1)
                else:
                    act.wait_ge(v_taken, g + 1)
                act.dma_start(a[:, cols].rearrange("(t p) n -> p t n", p=P), qkv_out[:, slot, 0:2]).then_inc(stored[slot], 16)
                act.dma_start(b[:, cols], qkv_out[:, slot, 2]).then_inc(stored[slot], 16)

            def qkv_group(g, first, last):
                W = W_QKV + 6 * g
                a = 8 + 3 * g
                if first:
                    mod_out(W, a, 6)
                else:
                    hi(W + 1, range(3)); mod_out(W, a, 6); hi(W + 1, [3])
                hi(W + 2, range(4)); square_heads(g, 0)
                hi(W + 3, range(3)); mod_out(W + 2, a + 1, 6); hi(W + 3, [3]); store(g, 0)
                hi(W + 4, range(4)); square_heads(g, 1)
                hi(W + 5, range(3)); mod_out(W + 4, a + 2, 6); hi(W + 5, [3]); store(g, 1)
                if not last:
                    hi(W + 6, range(4))
                act.wait_ge(sub_used, 4 * W + 24)
                act.wait_ge(stored[0], 64 * g + 32)
                act.activation(qkv_out[:, 0], bank[:, 0:3, :], ACT.Copy).then_inc(v_taken, 1)
                store(g, 2)

            qkv_group(0, True, False)
            with act.Fori(1, HG - 1) as g:
                qkv_group(g, False, False)
            qkv_group(HG - 1, False, True)

            def softplus_step(z, i):
                if i == 0:
                    step.mark(act.activation(e_buf[:], z, ACT.Abs))
                    return
                act.wait_ge(act_step, step.value())
                if i == 1:
                    step.mark(act.activation(e_buf[:], e_buf[:], ACT.Exp, scale=-1.0))
                else:
                    act.activation(e_buf[:], e_buf[:], ACT.Ln, bias=1.0).then_inc(ln_ready, 1)

            with loop(act, 0, HG, {step: 8}) as g:
                act.wait_ge(qkT_done, g + 1)
                act.activation(qT[:], bank[:, 0:4, 0:TOK], ACT.Copy).then_inc(qT_ready, 1)

                def keys_hi(b):
                    for i in range(2):
                        act.wait_ge(turned, 16 * g + 2 * b + i + 1)
                        if b >= 2:
                            act.wait_ge(kv_used, 16 * g + b - 1)
                        act.activation(s_hi[:, b % 2, 2 * i:2 * i + 2, :], bank[:, 4 + 2 * i:6 + 2 * i, :], ACT.Copy).then_inc(cache_hi, 1)

                def values_hi(b):
                    j = 8 + b
                    act.wait_ge(kv_loaded[j % 4], 64 * g + 16 * (j // 4) + 16)
                    for i in range(2):
                        if i == 0 and b >= 2:
                            act.wait_ge(half_used, 8 * g + b - 1)
                        else:
                            act.wait_ge(kv_used, 16 * g + j - 1)
                        act.activation(s_hi[:, j % 2, 2 * i:2 * i + 2, :], raw[:, j % 4, 2 * i:2 * i + 2, :], ACT.Copy).then_inc(cache_hi, 1)

                def query_hi(b):
                    if b >= 2:
                        act.wait_ge(kv_used, 16 * g + b - 1)
                    win = q_win[:, b % 2].rearrange("p (h c) -> p h c", c=WIN)
                    q = PROMPT + b * STEP
                    act.activation(win[:, :, 0:STEP], qT[:, :, q:q + STEP], ACT.Copy).then_inc(qhi_ready, 1)

                def scores_row(b):
                    act.wait_ge(kv_used, 16 * g + b + 1)
                    if b >= 2:
                        act.wait_ge(zpast_done, 8 * g + b - 1)
                    act.activation(z_row[:, b % 2], bank[:, 0, :], ACT.Copy, scale=SCALE).then_inc(zrow_ready, 1)

                def weights_hi(b):
                    act.wait_ge(w_ready, 4 * g + (2 if b < 4 else 4))
                    if b >= 2:
                        act.wait_ge(kv_used, 16 * g + 8 + b - 1)
                    else:
                        act.wait_ge(zself_done, g + 1)
                    act.activation(w_st[:, b % 2, :, 0:HQ], zs_past[:, b], ACT.Copy).then_inc(whi_ready, 1)

                def out_row(b):
                    act.wait_ge(kv_used, 16 * g + 8 + b + 1)
                    if b >= 2:
                        act.wait_ge(opast_done, 8 * g + b - 1)
                    act.activation(o_row[:, b % 2], bank[:, (4, 7)[b % 2], :], ACT.Copy).then_inc(orow_ready, 1)

                def self_rest(p, i):
                    if i == 0:
                        act.wait_ge(zself_taken, 2 * g + p + 1)
                        if p:
                            act.wait_ge(sp_ready, 4 * g + 1)
                    softplus_step(zs_self[:, 2 * p:2 * p + 2], i)

                def self_w(p):
                    act.wait_ge(t_ready, 4 * g + p + 1)
                    v = zs_self[:, 2 * p:2 * p + 2]
                    act.activation(v, v, ACT.Exp).then_inc(w_ready, 1)

                def self_hi(p):
                    act.wait_ge(oself_done, 2 * g + p + 1)
                    act.activation(h_hi[:, ds(g * 4 + 2 * p, 2), 0:PROMPT], bank[:, 0:2, 0:PROMPT], ACT.Copy).then_inc(ohi_ready, 1)

                def past_rest(q, i):
                    if i == 0:
                        act.wait_ge(zpast_taken, 8 * g + 4 * q + 4)
                        act.wait_ge(sp_ready, 4 * g + 2 + q)
                    softplus_step(half(zs_past, q), i)

                def past_w(q):
                    act.wait_ge(t_ready, 4 * g + 3 + q)
                    v = half(zs_past, q)
                    act.activation(v, v, ACT.Exp).then_inc(w_ready, 1)

                act.wait_ge(qT_ready, g + 1)
                keys_hi(0)
                act.wait_ge(win_clear, g + 1)
                query_hi(0); query_hi(1); self_rest(0, 0); self_rest(0, 1)
                keys_hi(1); self_rest(0, 2); scores_row(0); query_hi(2)
                keys_hi(2); scores_row(1); query_hi(3); self_rest(1, 0)
                keys_hi(3); self_rest(1, 1); scores_row(2); query_hi(4); self_rest(1, 2)
                keys_hi(4); scores_row(3); query_hi(5)
                keys_hi(5); scores_row(4); query_hi(6); self_w(0); past_rest(0, 0)
                keys_hi(6); past_rest(0, 1); scores_row(5); query_hi(7); past_rest(0, 2)
                keys_hi(7); scores_row(6); values_hi(0); scores_row(7)
                past_w(0); weights_hi(0); values_hi(1); weights_hi(1); self_w(1)
                past_rest(1, 0); past_rest(1, 1)
                out_row(0); values_hi(2); weights_hi(2); past_rest(1, 2); self_hi(0)
                out_row(1); values_hi(3); weights_hi(3)
                out_row(2); values_hi(4); past_w(1); weights_hi(4); self_hi(1)
                for b in range(5, STREAMS):
                    values_hi(b); out_row(b - 2); weights_hi(b)
                out_row(6)
                out_row(7)
                act.wait_ge(group_done, g + 2)
                act.activation(h_hi[:, ds(g * 4, 4), PROMPT:TOK], o_f[:], ACT.Copy).then_inc(ofhi_ready, 1)

            act.wait_ge(o_split, HG + 1)
            hi(W_O, range(4))
            for i in range(4):
                W = W_O + 2 * i
                hi(W + 1, range(4))
                hi(W + 2, range(3)); mod_out(W + 1, ADA_O + i, acc_bank(i)); hi(W + 2, [3])
            W = W_O + 8
            hi(W + 1, range(2)); mod_out(W, ADA_O + 4, acc_bank(4)); hi(W + 1, [2, 3])
            norm_stats(1)
            mod_out(W + 1, ADA_O + 5, acc_bank(5))
            norm_apply(1, BETWEEN_1)

            def ffn_chunk(W, c, with_ada, last=False, first=False):
                if with_ada:
                    a = ADA_FFN + 2 * c
                    if first:
                        hi(W + 1, [2]); mod_out(W, a, 4); hi(W + 1, [3])
                    else:
                        hi(W + 1, range(3)); mod_out(W, a, 4); hi(W + 1, [3])
                    W = W + 1
                hi(W + 1, range(3))
                act.wait_ge(sub_used, 4 * W + 4)
                act.activation(act_f[:], bank[:, 0:4, 0:TOK], ACT.Silu).then_inc(gate_taken, 1)
                hi(W + 1, [3])
                hi(W + 2, range(3))
                for m in range(4):
                    if with_ada and m == 3:
                        hi(W + 2, [3])
                    act.wait_ge(act_f_ready, 4 * c + m + 1)
                    act.activation(act_hi[:, m], act_f[:, m], ACT.Copy).then_inc(act_hi_ready, 1)
                if with_ada:
                    hi(W + 3, range(3)); mod_out(W + 2, a + 1, 0); hi(W + 3, [3])
                    hi(W + 4, range(4))
                else:
                    hi(W + 2, [3])
                    if not last:
                        hi(W + 3, range(4))

            ffn_chunk(W_FFN0, 0, True, first=True)
            with act.Fori(1, CHUNKS) as c:
                ffn_chunk(W_FFN0 + c * 5, c, True)

            norm_stats(2)

            def load_hist(j):
                if j >= 2:
                    act.wait_ge(hist_done, j - 1)
                act.dma_start(hrow[:, j % 2], hist_rows[:, 256 * j:256 * j + 256]).then_inc(hist_loaded[j % 2], 16)

            load_hist(0)
            load_hist(1)
            for j in range(8):
                act.wait_ge(hist_done, j + 1)
                hist = ext_views(ext)[2]
                act.wait_ge(xr_ready, XR[2] + j + 1)
                act.activation(hist, bank[:, 1, 0:240].rearrange("p (k b t) -> p k b t", k=2, b=STREAMS),
                               ACT.Copy).then_inc(hist_taken, 1)
                for k in range(2):
                    m = 2 * j + k
                    v = ext[:, k, STATE:STATE + PROMPT]
                    step.mark(act.activation(v, v, ACT.Identity, bias=modT[:, 1, SHIFT1 + m, 0:1], scale=coef[:, m, 0:1]))
                act.wait_ge(hs_ready, XR[2] + j + 1)
                act.activation(u_dense[:].rearrange("p k (b t) -> p k b t", b=STREAMS), ext_views(ext)[1], ACT.Copy).then_inc(u_ready, 1)
                if j + 2 < 8:
                    load_hist(j + 2)
                act.wait_ge(uT_done, j + 1)
                if j:
                    act.wait_ge(pool_stored, 144 * j)
                act.activation(urow[:], bank[:, 0, :].rearrange("p (t n) -> p t n", t=2), ACT.Copy).then_inc(uT_taken, 1)
                act.wait_ge(dif_ready, j + 1)
                dif = (sum_b, sum_a, sum_b, sum_a)[j // 2]
                act.activation(h_hi[:, 2 * j:2 * j + 2, :], dif[:, :, 0:TOK], ACT.Copy).then_inc(difhi_ready, 1)
            norm_stats(3)
            norm_apply(3, BETWEEN_3)

            with act.Fori(0, CHUNKS - 1) as c:
                ffn_chunk(W_FFN1 + c * 3, c + CHUNKS, False)
            ffn_chunk(W_FFN1 + 3 * (CHUNKS - 1), 2 * CHUNKS - 1, False, last=True)

            for i in range(1, 12, 2):
                t, q = i % TT, i // TT
                act.wait_ge(yT_done, i + 1)
                act.activation(yrow[:, t, q * 512:(q + 1) * 512], bank[:, i % 6], ACT.Copy).then_inc(y_act, 1)

        @block.vector
        def _(dve):
            step = Tally(dve_step)

            def own():
                dve.wait_ge(dve_step, step.value())

            def lo(W, subs):
                for s in subs:
                    dve.wait_ge(hi_ready, 4 * W + s + 1)
                    dve.tensor_tensor(w_lo[:, s], raw[:, s], w_hi[:, s].bitcast(f32), ALU.subtract).then_inc(lo_ready, 1)

            def mod_in(a, layer, j, t_bank):
                dve.wait_ge(ada_t, a + 1)
                bias = par[:, ds(MODT * layer + 4 * j, 4)].unsqueeze(2).to_broadcast([P, 4, NC])
                dve.tensor_tensor(modT[:, layer, ds(4 * j, 4), :],
                                  bank[:, t_bank, 0:4 * NC].rearrange("p (k c) -> p k c", k=4),
                                  bias, ALU.add).then_inc(ada_done, 1)

            def norm_coef(n):
                scale, _, gain, layer = norm_plan(n)
                dve.wait_ge(ada_done, (8, 20, 48, 48)[n])
                step.mark(dve.scalar_tensor_tensor(coef[:], modT[:, layer, scale:scale + KT, :], 1.0,
                                                   parG[:, gain:gain + KT].unsqueeze(2).to_broadcast([P, KT, NC]),
                                                   ALU.add, ALU.mult))

            def norm_root(n):
                stat_bank = STAT_BANK[n]
                for g in range(4):
                    dve.wait_ge(sq_ready, 4 * n + g + 1)
                    dve.tensor_reduce(sq_sum[:, g], nbuf[:, g % 2].rearrange("p k t -> p t k"), AX.X, ALU.add).then_inc(quad_summed, 1)
                dve.wait_ge(sq_used, n + 1)
                dve.tensor_scalar(rsb[:], bank[:, stat_bank, 0:TOK], 1.0 / D, EPS, ALU.mult, ALU.add).then_inc(var_ready, 1)
                dve.wait_ge(std_ready, n + 1)
                step.mark(dve.reciprocal(rsb[:], rsb[:]))
                own()

            def norm_apply(n, between=((), (), (), ())):
                _, shift, _, layer = norm_plan(n)
                for g in range(5):
                    if g < 4:
                        if g >= 2:
                            dve.wait_ge(h_ready, HR[n] + g - 1)
                        nb = nbuf[:, g % 2]
                        dve.tensor_tensor(nb, x[:, 4 * g:4 * g + 4, :], rsb[:].unsqueeze(1).to_broadcast([P, 4, TOK]),
                                          ALU.mult).then_inc(xr_ready, 1)
                        dve.wait_ge(xr_ready, XR[n] + g + 1)
                        s = nb[:, :, PROMPT:TOK].rearrange("p k (b t) -> p k b t", b=STREAMS)
                        step.mark(dve.tensor_tensor(s, s, per_stream(coef[:, 4 * g:4 * g + 4, :]), ALU.mult))
                        own()
                        m = shift + 4 * g
                        dve.tensor_tensor(s, s, per_stream(modT[:, layer, m:m + 4, :]), ALU.add).then_inc(hs_ready, 1)
                        for W, s in between[g]:
                            lo(W, [s])
                    if g:
                        dve.wait_ge(hhi_ready, HR[n] + g)
                        q = 4 * (g - 1)
                        dve.tensor_tensor(h_lo[:, q:q + 4, :], nbuf[:, (g - 1) % 2], h_hi[:, q:q + 4, :].bitcast(f32),
                                          ALU.subtract).then_inc(h_ready, 1)

            def add_quad(b0, m0, layer, gate):
                ps = bank[:, b0:b0 + 4, 0:TOK]
                mod = modT[:, layer, gate + m0:gate + m0 + 4, :]
                step.mark(dve.tensor_tensor(tmp_s[:].rearrange("p k (b t) -> p k b t", b=STREAMS),
                                            ps[:, :, PROMPT:TOK].rearrange("p k (b t) -> p k b t", b=STREAMS),
                                            per_stream(mod), ALU.mult))
                for k in range(4):
                    xv = x[:, m0 + k, 0:PROMPT]
                    step.mark(dve.scalar_tensor_tensor(xv, ps[:, k, 0:PROMPT], mod[:, k, 0:1], xv, ALU.mult, ALU.add))
                own()
                xs = x[:, m0:m0 + 4, PROMPT:TOK]
                dve.tensor_tensor(xs, xs, tmp_s[:], ALU.add).then_inc(residual_taken, 1)
            ADD = 5

            dve.memset(c18[:, KT * C18:].bitcast(f32), 0.0).then_inc(c18_ready, 1)
            dve.wait_ge(const_ready, 1)
            for i, w in enumerate(WINDOWS):
                step.mark(dve.tensor_scalar(icount[:, i], icount[:, i], float(w), None, ALU.min))
            own()
            step.mark(dve.reciprocal(icount[:], icount[:]))
            dve.wait_ge(cT_done, 1)
            cT = bank[:, 6, 0:KT * NC].rearrange("p (k c) -> p k c", c=NC)
            dve.tensor_copy(c_hi[:, :, 0:NC], cT).then_inc(c18_ready, 1)
            dve.wait_ge(c18_ready, 2)
            dve.tensor_tensor(c_hi[:, :, NC:C18], cT, c_hi[:, :, 0:NC].bitcast(f32), ALU.subtract).then_inc(c18_ready, 1)
            lo(0, range(4))
            dve.wait_ge(parT_done, 1)
            dve.tensor_copy(par[:], bank[:, 7, 0:2 * MODT + 5 * KT]).then_inc(par_ready, 1)
            lo(1, range(3))
            for i in range(0, 12, 2):
                t, q = i // 4, i % 4
                dve.wait_ge(xT_done, i + 1)
                dve.tensor_copy(x[:, 4 * q:4 * q + 4, t * P:(t + 1) * P],
                                bank[:, i % 6].rearrange("p (k c) -> p k c", k=4)).then_inc(xT_dve, 1)
            dve.wait_ge(par_ready, 1)
            mod_in(0, 0, 0, 7)
            lo(1, [3])
            norm_root(0)
            with loop(dve, 1, 8, {}) as a:
                lo(a + 1, range(3))
                mod_in(a, 0, a, 7)
                lo(a + 1, [3])
            norm_coef(0)
            own()
            norm_apply(0, BETWEEN_0)
            dve.wait_ge(gqk_loaded, 32)

            def norm_heads(g, i, W):
                b0 = 3 * i
                r = qk_rs[:, i]
                ps = bank[:, b0:b0 + 3, :].rearrange("p t (h d) -> p t h d", d=HD)
                out = qkv_out[:, i].rearrange("p t (h d) -> p t h d", d=HD)
                lo(W, [0])
                dve.wait_ge(qksq_ready, 2 * g + i + 1)
                step.mark(dve.tensor_reduce(r.rearrange("p (t h) -> p t h", t=3), sq[:].rearrange("p t (h d) -> p t h d", d=HD), AX.X, ALU.add))
                own()
                dve.tensor_scalar(r, r, 1.0 / HD, EPS, ALU.mult, ALU.add).then_inc(qkvar_ready, 1)
                gain = gqk[:, i].unsqueeze(1).unsqueeze(1).to_broadcast([P, TT, 4, HD])
                lo(W, [1])
                dve.tensor_tensor(out, ps, gain, ALU.mult).then_inc(qk_taken, 1)
                dve.wait_ge(qkrs_ready, 2 * g + i + 1)
                dve.wait_ge(qk_taken, 2 * g + i + 1)
                dve.tensor_tensor(out, out, r.rearrange("p (t h) -> p t h", t=3).unsqueeze(3).to_broadcast([P, TT, 4, HD]),
                                  ALU.mult).then_inc(qk_ready, 1)

            def qkv_group(g, first, last):
                W = W_QKV + 6 * g
                a = 8 + 3 * g
                if not first:
                    lo(W + 1, range(4))
                lo(W + 2, [0]); mod_in(a, 0, a, 7); lo(W + 2, range(1, 4))
                if not first:
                    dve.wait_ge(stored[0], 64 * g)
                norm_heads(g, 0, W + 3)
                lo(W + 3, [2, 3])
                lo(W + 4, [0]); mod_in(a + 1, 0, a + 1, 7); lo(W + 4, range(1, 4))
                if not first:
                    dve.wait_ge(stored[1], 32 * g)
                norm_heads(g, 1, W + 5)
                lo(W + 5, [2, 3])
                if not last:
                    lo(W + 6, [0]); mod_in(a + 2, 0, a + 2, 7); lo(W + 6, range(1, 4))
                else:
                    mod_in(a + 2, 0, a + 2, 7)

            qkv_group(0, True, False)
            with loop(dve, 1, HG - 1, {step: 2}) as g:
                qkv_group(g, False, False)
            qkv_group(HG - 1, False, True)

            dve.wait_ge(v_taken, HG)
            dve.wait_ge(mod_ready, ADA_O)
            dve.wait_ge(const_ready, 1)
            dve.memset(tmp_s[:, 0, 0:1], 0.0).then_inc(group_done, 1)
            dve.memset(tmp_s[:, 0, 1:2], 0.0).then_inc(o_split, 1)
            dve.wait_ge(stored[0], 16 * 4 * HG)
            dve.wait_ge(stored[1], 16 * 2 * HG)

            with loop(dve, 0, HG, {step: 8}) as g:
                dve.wait_ge(kturn_done, g + 1)
                dve.tensor_copy(kT[:], bank[:, 4:8, 0:TOK]).then_inc(kT_ready, 1)
                dve.wait_ge(kT_ready, g + 1)
                dve.wait_ge(qkT_done, g + 1)
                dve.memset(q_win[:].bitcast(f32), 0.0).then_inc(win_clear, 1)

                def cache_rest(j):
                    for i in range(2):
                        dve.wait_ge(cache_hi, 32 * g + 2 * j + i + 1)
                        if j < 8:
                            dve.wait_ge(turned, 16 * g + 2 * j + 2)
                            src = bank[:, 4 + 2 * i:6 + 2 * i, :]
                        else:
                            src = raw[:, j % 4, 2 * i:2 * i + 2, :]
                        dve.tensor_tensor(s_lo[:, j % 4, 2 * i:2 * i + 2, :], src, s_hi[:, j % 2, 2 * i:2 * i + 2, :].bitcast(f32),
                                          ALU.subtract).then_inc(cache_lo, 1)

                def query_lo(b):
                    dve.wait_ge(qhi_ready, 8 * g + b + 1)
                    win = q_win[:, b % 2].rearrange("p (h c) -> p h c", c=WIN)
                    q = PROMPT + b * STEP
                    dve.tensor_tensor(win[:, :, HQ:HQ + STEP], qT[:, :, q:q + STEP], win[:, :, 0:STEP].bitcast(f32),
                                      ALU.subtract).then_inc(q_split, 1)

                def scores_out(b):
                    dve.wait_ge(zpast_done, 8 * g + b + 1)
                    dve.tensor_reduce(zs_past[:, b], bank[:, 1, :].rearrange("p (k r n) -> p k n r", k=PKT, r=2),
                                      AX.X, ALU.add).then_inc(zpast_taken, 1)

                def out_past(b):
                    dve.wait_ge(opast_done, 8 * g + b + 1)
                    c = (5 + b % 2) * 512
                    own_head = bank[:].rearrange("p a n -> p (a n)")[:, c:c + 4 * WIN].rearrange("p (h c) -> p h c", c=WIN)
                    parts = own_head[:, :, 0:P].rearrange("p h (r n) -> p h n r", r=2)[:, :, 0:STEP, :]
                    dve.tensor_reduce(o_f[:, :, b * STEP:(b + 1) * STEP], parts, AX.X, ALU.add).then_inc(opast_taken, 1)

                def self_scores(p):
                    dve.wait_ge(zself_done, g + 1)
                    pair = slice(2 * p, 2 * p + 2)
                    dve.scalar_tensor_tensor(zs_self[:, pair], bank[:, pair, :], SCALE, mask[:].unsqueeze(1).to_broadcast([P, 2, 512]),
                                             ALU.mult, ALU.min).then_inc(zself_taken, 1)

                def self_sp(p):
                    dve.wait_ge(ln_ready, 4 * g + p + 1)
                    if p:
                        dve.wait_ge(tri_done, 4 * g + 1)
                        own()
                    dve.scalar_tensor_tensor(sp_buf[:], zs_self[:, 2 * p:2 * p + 2], 0.0, e_buf[:], ALU.max, ALU.add).then_inc(sp_ready, 1)
                    dve.wait_ge(sp_ready, 4 * g + p + 1)
                    step.mark(dve.tensor_copy(later[:, :, PKT - 1, 2 * p * STEP:(2 * p + 2) * STEP].rearrange("p b (i t) -> p b i t", i=2),
                                              sp_buf[:, :, 384:512].rearrange("p i (b t) -> p b i t", b=STREAMS)))

                def self_t(p):
                    dve.wait_ge(tri_done, 4 * g + p + 1)
                    v = zs_self[:, 2 * p:2 * p + 2]
                    dve.tensor_tensor(v, v, bank[:, 2:4, :], ALU.subtract).then_inc(t_ready, 1)

                def self_out(p):
                    dve.wait_ge(oself_done, 2 * g + p + 1)
                    dve.wait_ge(ohi_ready, 2 * g + p + 1)
                    step.mark(dve.tensor_copy(o_new[:, 2 * p:2 * p + 2, :], bank[:, 0:2, PROMPT:TOK]))
                    k = ds(g * 4 + 2 * p, 2)
                    dve.tensor_tensor(h_lo[:, k, 0:PROMPT], bank[:, 0:2, 0:PROMPT], h_hi[:, k, 0:PROMPT].bitcast(f32),
                                      ALU.subtract).then_inc(oself_taken, 1)

                def past_sp(q):
                    dve.wait_ge(ln_ready, 4 * g + 3 + q)
                    dve.wait_ge(tri_done, 4 * g + 2 + q)
                    own()
                    dve.scalar_tensor_tensor(sp_buf[:], half(zs_past, q), 0.0, e_buf[:], ALU.max, ALU.add).then_inc(sp_ready, 1)
                    dve.wait_ge(sp_ready, 4 * g + 3 + q)
                    l = later[:, 4 * q:4 * q + 4]
                    sp = sp_buf[:].rearrange("p i (b k n) -> p (i b) k n", b=2, k=PKT)
                    for k in (2, 1, 0):
                        ins = dve.tensor_tensor(l[:, :, k, :], l[:, :, k + 1, :], sp[:, :, k + 1, :], ALU.add)
                        if k:
                            step.mark(ins)
                            own()
                        else:
                            ins.then_inc(later_ready, 1)

                def past_t(q):
                    dve.wait_ge(tri_done, 4 * g + 3 + q)
                    z = half(zs_past, q)
                    dve.tensor_tensor(z, z, bank[:, 2:4, :], ALU.subtract).then_inc(t_ready, 1)

                cache_rest(0)
                self_scores(0); query_lo(0); query_lo(1)
                cache_rest(1); self_scores(1); query_lo(2); self_sp(0)
                cache_rest(2); query_lo(3); scores_out(0)
                cache_rest(3); query_lo(4); self_t(0); scores_out(1); self_sp(1)
                cache_rest(4); query_lo(5); scores_out(2)
                cache_rest(5); query_lo(6); scores_out(3); self_t(1)
                cache_rest(6); query_lo(7); scores_out(4); past_sp(0)
                cache_rest(7); scores_out(5); past_t(0); scores_out(6)
                cache_rest(8); scores_out(7)
                dve.wait_ge(o_split, g + 1)
                cache_rest(9)
                cache_rest(10); out_past(0); past_sp(1); self_out(0)
                cache_rest(11); past_t(1); out_past(1)
                cache_rest(12); out_past(2); self_out(1)
                for b in range(5, STREAMS):
                    cache_rest(8 + b); out_past(b - 2)
                out_past(6)
                out_past(7)
                dve.wait_ge(opast_taken, 8 * g + 8)
                dve.wait_ge(oself_taken, 2 * g + 2)
                dve.tensor_tensor(o_f[:], o_f[:], o_new[:], ALU.add).then_inc(group_done, 1)
                dve.wait_ge(ofhi_ready, g + 1)
                k = ds(g * 4, 4)
                dve.tensor_tensor(h_lo[:, k, PROMPT:TOK], o_f[:], h_hi[:, k, PROMPT:TOK].bitcast(f32), ALU.subtract).then_inc(o_split, 1)

            own()
            lo(W_O, range(4))
            for i in range(4):
                W = W_O + 2 * i
                lo(W + 1, range(4))
                dve.wait_ge(sub_used, 4 * W + 4)
                if i:
                    dve.wait_ge(residual_taken, i)
                add_quad(4 * (i % 2), 4 * i, 0, GATE1)
                lo(W + 2, [0]); mod_in(ADA_O + i, 0, ADA_O + i, acc_bank(i) + 1); lo(W + 2, range(1, 4))
            W = W_O + 8
            lo(W + 1, range(3)); mod_in(ADA_O + 4, 1, 0, acc_bank(4) + 1); lo(W + 1, [3])
            norm_coef(1)
            norm_root(1)
            mod_in(ADA_O + 5, 1, 1, acc_bank(5) + 1)
            norm_apply(1, BETWEEN_1)

            def ffn_chunk(W, c, layer, r, with_ada, last=False, first=False):
                if with_ada:
                    a = ADA_FFN + 2 * c
                    j = 2 * c + (ADA_FFN - 24)
                    lo(W + 1, [2, 3] if first else range(4))
                    lo(W + 2, [0]); mod_in(a, 1, j, 5); lo(W + 2, range(1, 4))
                    W = W + 1
                else:
                    lo(W + 1, range(4))
                lo(W + 2, range(3))
                dve.wait_ge(gate_taken, c + 1)
                for m in range(4):
                    if m < 3:
                        dve.wait_ge(up_tile, 3 * c + m + 1)
                    else:
                        dve.wait_ge(sub_used, 4 * W + 8)
                    dve.tensor_tensor(act_f[:, m], act_f[:, m], bank[:, 4 + m, 0:TOK], ALU.mult).then_inc(act_f_ready, 1)
                if with_ada:
                    lo(W + 2, [3])
                    down = W + 3
                    lo(down, range(4))
                else:
                    lo(W + 2, [3])
                    down = W + 2
                for s in range(4):
                    if not last and not with_ada:
                        lo(down + 1, [s])
                    if with_ada and s == 0:
                        mod_in(a + 1, 1, j + 1, 3)
                    dve.wait_ge(sub_used, 4 * down + s + 1)
                    dve.wait_ge(residual_taken, r + s)
                    add_quad(down_bank(s, with_ada), 4 * s, layer, GATE2)
                    if with_ada:
                        lo(down + 1, [s])

            ffn_chunk(W_FFN0, 0, 0, R_FFN0, True, first=True)
            with loop(dve, 1, CHUNKS, {step: 4 * ADD}) as c:
                ffn_chunk(W_FFN0 + c * 5, c, 0, R_FFN0 + c * 4, True)

            norm_coef(2)
            norm_root(2)
            gate = modT[:, 1, GATE1:GATE1 + KT, :]
            step.mark(dve.tensor_tensor(gate, gate, parG[:, 4 * KT:5 * KT].unsqueeze(2).to_broadcast([P, KT, NC]), ALU.mult))
            def pooled(s):
                dve.wait_ge(sub_used, 4 * W_POOL + s + 1)
                dve.wait_ge(residual_taken, R_POOL + s)
                add_quad(4, 4 * s, 1, GATE1)

            u_p, u_s, _ = ext_views(ext)

            def mixer_input(j):
                own()
                if j:
                    dve.wait_ge(dif_ready, j)
                    dve.wait_ge(uT_done, j)
                xp, xs = quads(x, 2 * j, 2)
                if j == 0:
                    step.mark(dve.memset(ext[:, :, 0:STATE], 0.0))
                step.mark(dve.tensor_tensor(u_p, xp, rsb[:, 0:PROMPT].unsqueeze(1).to_broadcast([P, 2, PROMPT]), ALU.mult))
                rs_s = rsb[:, PROMPT:TOK].rearrange("p (b t) -> p b t", b=STREAMS).unsqueeze(1).to_broadcast([P, 2, STREAMS, STEP])
                dve.tensor_tensor(u_s, xs, rs_s, ALU.mult).then_inc(xr_ready, 1)
                dve.wait_ge(xr_ready, 8 + j + 1)
                step.mark(dve.tensor_tensor(u_s, u_s, per_stream(coef[:, 2 * j:2 * j + 2, :], 2), ALU.mult))
                own()
                dve.tensor_tensor(u_s, u_s, per_stream(modT[:, 1, SHIFT1 + 2 * j:SHIFT1 + 2 * j + 2, :], 2), ALU.add).then_inc(hs_ready, 1)

            mixer_input(0)
            for j in range(8):
                g, w = j // 2, WINDOWS[j // 2]
                dve.wait_ge(hs_ready, 8 + j + 1)
                dve.wait_ge(hist_taken, j + 1)
                dve.wait_ge(u_ready, j + 1)
                if j:
                    dve.wait_ge(dif_split, j)
                src, span = ext, 1
                for dst in (sum_a, sum_b, sum_a, sum_b)[:g + 1]:
                    n0 = 2 * span - 1
                    step.mark(dve.tensor_tensor(dst[:, :, n0:EXT], src[:, :, n0:EXT], src[:, :, n0 - span:EXT - span], ALU.add))
                    own()
                    src, span = dst, 2 * span
                s_p, s_s, _ = ext_views(src)
                dif = sum_b if src is sum_a else sum_a
                d_p = dif[:, :, 0:PROMPT]
                d_s = dif[:, :, PROMPT:TOK].rearrange("p k (b t) -> p k b t", b=STREAMS)
                for k in range(2):
                    step.mark(dve.scalar_tensor_tensor(d_s[:, k], s_s[:, k], 1.0 / w, u_s[:, k], ALU.mult, ALU.subtract))
                step.mark(dve.scalar_tensor_tensor(d_p[:, :, 16:], s_p[:, :, 16:], 1.0 / w, u_p[:, :, 16:], ALU.mult, ALU.subtract))
                step.mark(dve.tensor_tensor(d_p[:, :, 0:16], s_p[:, :, 0:16], icount[:, g].unsqueeze(1).to_broadcast([P, 2, 16]), ALU.mult))
                own()
                dve.tensor_tensor(d_p[:, :, 0:16], d_p[:, :, 0:16], u_p[:, :, 0:16], ALU.subtract).then_inc(dif_ready, 1)
                if j < 7:
                    mixer_input(j + 1)
                if j >= 3 and j % 2:
                    pooled(g - 1)
            pooled(3)
            dve.wait_ge(pool_stored, 16 * 9 * 8)
            norm_coef(3)
            norm_root(3)
            norm_apply(3, BETWEEN_3)
            with loop(dve, 0, CHUNKS - 1, {step: 4 * ADD}) as c:
                ffn_chunk(W_FFN1 + c * 3, c + CHUNKS, 1, R_FFN1 + c * 4, False)
            ffn_chunk(W_FFN1 + 3 * (CHUNKS - 1), 2 * CHUNKS - 1, 1, R_FFN1 + 4 * (CHUNKS - 1), False, last=True)

            for i in range(0, 12, 2):
                t, q = i % TT, i // TT
                dve.wait_ge(yT_done, i + 1)
                dve.tensor_copy(yrow[:, t, q * 512:(q + 1) * 512], bank[:, i % 6]).then_inc(y_dve, 1)

        @block.tensor
        def _(pe):
            def product(out, w, wl, a, al, start, stop):
                pe.matmul(out, w, a, start=start, stop=False)
                pe.matmul(out, w, al, start=False, stop=False)
                return pe.matmul(out, wl, a, start=False, stop=stop)

            def ada_block(W, a, acc_bank, first=False):
                if not first:
                    pe.wait_ge(mod_ready, a)
                for s in range(4):
                    pe.wait_ge(lo_ready, 4 * W + s + 1)
                    for k in range(4):
                        kt = 4 * s + k
                        lhs = c18[:, kt * C18:kt * C18 + 66]
                        pe.matmul(bank[0:66, acc_bank, :], lhs, w_hi[:, s, k], start=(kt == 0), stop=False)
                        last = pe.matmul(bank[0:66, acc_bank, :], lhs, w_lo[:, s, k], start=False, stop=(kt == KT - 1))
                    last.then_inc(sub_used, 1)

            def ada_turn(a, t_bank, first=False):
                pe.wait_ge(mod_ready, a + 1)
                if not first:
                    pe.wait_ge(ada_done, a)
                for t in range(4):
                    last = pe.matmul(bank[:, t_bank, t * NC:(t + 1) * NC], mod18[:, t * P:(t + 1) * P], fold[:], start=True, stop=True)
                last.then_inc(ada_t, 1)

            def norm_stats(n):
                stat_bank = STAT_BANK[n]
                for g in range(4):
                    pe.wait_ge(quad_summed, 4 * n + g + 1)
                    last = pe.matmul(bank[:, stat_bank, 0:TOK], ones[:], sq_sum[:, g], start=(g == 0), stop=(g == 3))
                last.then_inc(sq_used, 1)

            def to_features(W, s, b0, act_h, act_l, k0, start, stop):
                pe.wait_ge(lo_ready, 4 * W + s + 1)
                for k in range(4):
                    for m in range(4):
                        cols = slice(m * P, (m + 1) * P)
                        last = product(bank[:, b0 + m, 0:TOK], w_hi[:, s, k, cols], w_lo[:, s, k, cols],
                                       act_h[:, k0 + k, :], act_l[:, k0 + k, :], start and k == 0, stop and k == 3)
                last.then_inc(sub_used, 1)

            def to_tokens(W, b0, a):
                for s in range(4):
                    pe.wait_ge(lo_ready, 4 * W + s + 1)
                    pe.wait_ge(h_ready, s + 1)
                    for k in range(4):
                        kt = 4 * s + k
                        for t in range(TT):
                            cols = slice(t * P, (t + 1) * P)
                            out = bank[:, b0 + t, :]
                            pe.matmul(out, h_hi[:, kt, cols], w_hi[:, s, k], start=(kt == 0), stop=False)
                            pe.matmul(out, h_hi[:, kt, cols], w_lo[:, s, k], start=False, stop=False)
                            last = pe.matmul(out, h_lo[:, kt, cols], w_hi[:, s, k], start=False, stop=(kt == KT - 1))
                    last.then_inc(sub_used, 1)
                    if s == 0:
                        ada_turn(a, 7)

            pe.wait_ge(const_ready, 1)
            pe.wait_ge(silu_c, 1)
            for k in range(KT):
                last = pe.transpose(bank[:, 6, k * NC:(k + 1) * NC], csil[:, k * P:(k + 1) * P], ident[0:NC, 0:NC])
            last.then_inc(cT_done, 1)
            pe.wait_ge(c18_ready, 3)
            ada_block(0, 0, 6, first=True)
            pe.wait_ge(par_loaded, 16 * 7)
            for i, n in enumerate((96, 96, 80)):
                last = pe.transpose(bank[:, 7, i * 96:i * 96 + n], prow[0:n, i], ident[0:n, 0:n])
            last.then_inc(parT_done, 1)
            pe.wait_ge(x_loaded, 16 * TT)
            for i in range(12):
                t, q = i // 4, i % 4
                if i >= 6:
                    pe.wait_ge(xT_act if i % 2 else xT_dve, (i - 6) // 2 + 1)
                for k in range(4):
                    c = (4 * q + k) * P
                    last = pe.transpose(bank[:, i % 6, k * P:(k + 1) * P], xrow[:, t, c:c + P], ident[:])
                last.then_inc(xT_done, 1)

            pe.wait_ge(par_ready, 1)
            ada_turn(0, 7, first=True)
            pe.wait_ge(xT_dve, 6)
            pe.wait_ge(xT_act, 6)
            norm_stats(0)
            with pe.Fori(1, 8) as a:
                ada_block(a, a, 6)
                ada_turn(a, 7)

            def qkv_group(g, first):
                W = W_QKV + 6 * g
                a = 8 + 3 * g
                ada_block(W, a, 6)
                if not first:
                    pe.wait_ge(v_taken, g)
                to_tokens(W + 1, 0, a)
                ada_block(W + 2, a + 1, 6)
                if not first:
                    pe.wait_ge(qk_taken, 2 * g)
                to_tokens(W + 3, 3, a + 1)
                ada_block(W + 4, a + 2, 6)
                pe.wait_ge(qk_taken, 2 * g + 1)
                to_tokens(W + 5, 0, a + 2)

            qkv_group(0, True)
            with pe.Fori(1, HG) as g:
                qkv_group(g, False)

            with pe.Fori(0, HG) as g:
                pe.wait_ge(tok_loaded, 80 * g + 80)
                pe.wait_ge(group_done, g + 1)
                for i, done in ((1, kturn_done), (0, qkT_done)):
                    for h in range(4):
                        for t in range(TT):
                            last = pe.transpose(bank[:, 4 * i + h, t * P:(t + 1) * P],
                                                tok[:, i, t, h * HD:(h + 1) * HD], ident[:])
                    last.then_inc(done, 1)

                def turn_keys(b):
                    pe.wait_ge(kv_loaded[b % 4], 64 * g + 16 * (b // 4) + 16)
                    for i in range(2):
                        if b:
                            pe.wait_ge(cache_lo, 32 * g + 2 * b - 1 + i)
                        for h in (2 * i, 2 * i + 1):
                            for k in range(PKT):
                                last = pe.transpose(bank[:, 4 + h, k * P:(k + 1) * P], raw[:, b % 4, k, h * HD:(h + 1) * HD], ident[:])
                        last.then_inc(turned, 1)

                def past_scores(b):
                    pe.wait_ge(cache_lo, 32 * g + 2 * b + 2)
                    pe.wait_ge(q_split, 8 * g + b + 1)
                    if b:
                        pe.wait_ge(zrow_ready, 8 * g + b)
                    else:
                        pe.wait_ge(zself_taken, 2 * g + 1)
                    for h in range(4):
                        win = q_win[:, b % 2, h * P:(h + 1) * P]
                        pe.matmul(bank[:, 0, :], win, s_hi[:, b % 2, h], start=(h == 0), stop=False)
                        last = pe.matmul(bank[:, 0, :], win, s_lo[:, b % 4, h], start=False, stop=(h == 3))
                    last.then_inc(kv_used, 1)

                def turn_scores(b):
                    pe.wait_ge(zrow_ready, 8 * g + b + 1)
                    if b:
                        pe.wait_ge(zpast_taken, 8 * g + b)
                    for k in range(PKT):
                        last = pe.transpose(bank[:, 1, k * P:(k + 1) * P], z_row[:, b % 2, k * P:(k + 1) * P], ident[:])
                    last.then_inc(zpast_done, 1)

                def past_sums(q):
                    pe.wait_ge(later_ready, 2 * g + q + 1)
                    pe.wait_ge(t_ready, 4 * g + 2 + q)
                    for i in range(2):
                        pe.matmul(bank[:, 2 + i, :], tri[:], sp_buf[:, i, :], start=True, stop=False)
                        last = pe.matmul(bank[:, 2 + i, :], ones[:], half(later, q)[:, i], start=False, stop=True)
                    last.then_inc(tri_done, 1)

                def past_values(b):
                    j = 8 + b
                    pe.wait_ge(cache_lo, 32 * g + 2 * j + 2)
                    pe.wait_ge(w_split, 8 * g + b + 1)
                    if b >= 2:
                        pe.wait_ge(orow_ready, 8 * g + b - 1)
                    out = bank[:, (4, 7)[b % 2], :]
                    for k in range(PKT):
                        pe.matmul(out, w_st[:, b % 2, k], s_hi[:, j % 2, k], start=(k == 0), stop=False)
                        last = pe.matmul(out, w_st[:, b % 2, k], s_lo[:, j % 4, k], start=False, stop=(k == PKT - 1))
                        if k == 1:
                            last.then_inc(half_used, 1)
                    last.then_inc(kv_used, 1)

                def turn_out(b):
                    pe.wait_ge(orow_ready, 8 * g + b + 1)
                    if b >= 2:
                        pe.wait_ge(opast_taken, 8 * g + b - 1)
                    for h in range(4):
                        last = pe.transpose(bank[:, 5 + b % 2, h * P:(h + 1) * P], o_row[:, b % 2, h * P:(h + 1) * P], ident[:])
                    last.then_inc(opast_done, 1)

                def self_sums(p):
                    pe.wait_ge(sp_ready, 4 * g + p + 1)
                    if p:
                        pe.wait_ge(t_ready, 4 * g + 1)
                    else:
                        pe.wait_ge(zself_taken, 2 * g + 2)
                    for i in range(2):
                        pe.matmul(bank[:, 2 + i, :], tri[:], sp_buf[:, i, :], start=True, stop=False)
                        last = pe.matmul(bank[:, 2 + i, P:2 * P], ones[:], sp_buf[:, i, 256:384], start=False, stop=True)
                    last.then_inc(tri_done, 1)

                def self_values(p):
                    pe.wait_ge(w_ready, 4 * g + 2 * p + 1)
                    if p:
                        pe.wait_ge(oself_taken, 2 * g + 1)
                    for i in range(2):
                        h = 2 * p + i
                        if i and not p:
                            pe.wait_ge(zpast_taken, 8 * g + 8)
                        v = [tok[:, 2, t, h * HD:(h + 1) * HD] for t in range(TT)]
                        b = bank[:, i]
                        pe.matmul(b[:, 256:384], v[2], zs_self[:, h, 384:512], start=True, stop=True)
                        pe.matmul(b[:, 0:256], v[0], zs_self[:, h, 0:256], start=True, stop=False)
                        last = pe.matmul(b[:, P:256], v[1], zs_self[:, h, 256:384], start=False, stop=True)
                    last.then_inc(oself_done, 1)

                pe.wait_ge(kT_ready, g + 1)
                turn_keys(0)
                pe.wait_ge(qT_ready, g + 1)
                for h in range(4):
                    pe.matmul(bank[:, h, 0:256], kT[:, h, 0:P], qT[:, h, 0:256], start=True, stop=True)
                    pe.matmul(bank[:, h, 256:384], kT[:, h, P:2 * P], qT[:, h, P:2 * P], start=True, stop=True)
                    last = pe.matmul(bank[:, h, 384:512], kT[:, h, 2 * P:3 * P], qT[:, h, 2 * P:3 * P], start=True, stop=True)
                last.then_inc(zself_done, 1)
                turn_keys(1); past_scores(0)
                turn_keys(2); past_scores(1); turn_scores(0); self_sums(0)
                turn_keys(3); past_scores(2); turn_scores(1)
                turn_keys(4); past_scores(3); turn_scores(2); self_sums(1)
                turn_keys(5); past_scores(4); turn_scores(3)
                turn_keys(6); past_scores(5); turn_scores(4)
                turn_keys(7); past_scores(6); turn_scores(5); past_sums(0)
                past_scores(7); turn_scores(6); turn_scores(7)
                self_values(0); past_values(0)
                past_values(1); turn_out(0)
                past_values(2); turn_out(1); past_sums(1)
                past_values(3); turn_out(2); self_values(1)
                for b in range(4, STREAMS):
                    past_values(b); turn_out(b - 1)
                turn_out(STREAMS - 1)

            pe.wait_ge(o_split, HG + 1)
            for i in range(4):
                W = W_O + 2 * i
                if i:
                    pe.wait_ge(ada_done, ADA_O + i)
                for s in range(4):
                    to_features(W, s, 4 * (i % 2), h_hi, h_lo, 4 * s, s == 0, s == 3)
                if i:
                    pe.wait_ge(residual_taken, i)
                ada_block(W + 1, ADA_O + i, acc_bank(i))
                ada_turn(ADA_O + i, acc_bank(i) + 1)
            W = W_O + 8
            pe.wait_ge(residual_taken, 4)
            ada_block(W, ADA_O + 4, acc_bank(4))
            ada_turn(ADA_O + 4, acc_bank(4) + 1)
            ada_block(W + 1, ADA_O + 5, acc_bank(5))
            norm_stats(1)
            ada_turn(ADA_O + 5, acc_bank(5) + 1)

            def ffn_chunk(W, c, r, hr, with_ada):
                if with_ada:
                    a = ADA_FFN + 2 * c
                    pe.wait_ge(residual_taken, r - 1)
                    ada_block(W, a, 4)
                    W = W + 1
                pe.wait_ge(residual_taken, r if with_ada else r - 1)
                for s in range(4):
                    pe.wait_ge(h_ready, hr + s + 1)
                    to_features(W, s, 0, h_hi, h_lo, 4 * s, s == 0, s == 3)
                    if with_ada and s == 0:
                        ada_turn(a, 5)
                if with_ada:
                    pe.wait_ge(ada_done, a + 1)
                else:
                    pe.wait_ge(residual_taken, r)
                for s in range(3):
                    to_features(W + 1, s, 4, h_hi, h_lo, 4 * s, s == 0, False)
                pe.wait_ge(lo_ready, 4 * W + 8)
                for m in range(4):
                    cols = slice(m * P, (m + 1) * P)
                    for k in range(4):
                        last = product(bank[:, 4 + m, 0:TOK], w_hi[:, 3, k, cols], w_lo[:, 3, k, cols],
                                       h_hi[:, 12 + k, :], h_lo[:, 12 + k, :], False, k == 3)
                    last.then_inc(up_tile if m < 3 else sub_used, 1)
                down = W + 2
                if with_ada:
                    pe.wait_ge(gate_taken, c + 1)
                    ada_block(W + 2, a + 1, 0)
                    down = W + 3
                for s in range(4):
                    if s == 0:
                        pe.wait_ge(lo_ready, 4 * down + 1)
                        for k in range(4):
                            if k == 0 and with_ada:
                                pe.wait_ge(act_ready, 4 * c + 4)
                            elif not with_ada:
                                pe.wait_ge(act_ready, 4 * c + k + 1)
                            if k == 2 and with_ada:
                                ada_turn(a + 1, 3)
                            for m in range(4):
                                cols = slice(m * P, (m + 1) * P)
                                last = product(bank[:, down_bank(0, with_ada) + m, 0:TOK], w_hi[:, 0, k, cols], w_lo[:, 0, k, cols],
                                               act_hi[:, k, :], act_lo[:, k, :], k == 0, k == 3)
                        last.then_inc(sub_used, 1)
                    else:
                        if s == 1:
                            if with_ada:
                                pe.wait_ge(ada_done, a + 2)
                            else:
                                pe.wait_ge(act_ready, 4 * c + 4)
                        if s >= 2:
                            pe.wait_ge(residual_taken, r + s - 1)
                        to_features(down, s, down_bank(s, with_ada), act_hi, act_lo, 0, True, True)

            with pe.Fori(0, CHUNKS) as c:
                ffn_chunk(W_FFN0 + c * 5, c, R_FFN0 + c * 4, 4, True)

            pe.wait_ge(residual_taken, R_POOL)
            norm_stats(2)
            u_p, u_s, _ = ext_views(ext)

            def turn_history(j):
                pe.wait_ge(hist_loaded[j % 2], 16 * (j // 2 + 1))
                if j:
                    pe.wait_ge(hist_taken, j)
                for k in range(2):
                    last = pe.transpose(bank[:, 1, 120 * k:120 * (k + 1)], hrow[:, j % 2, k * P:(k + 1) * P], ident[0:120, 0:120])
                last.then_inc(hist_done, 1)

            def map_group(s):
                pe.wait_ge(dif_split, 2 * s + 2)
                if s:
                    pe.wait_ge(residual_taken, R_POOL + s)
                to_features(W_POOL, s, 4, h_hi, h_lo, 4 * s, True, True)

            turn_history(0)
            for j in range(8):
                pe.wait_ge(u_ready, j + 1)
                if j:
                    pe.wait_ge(uT_taken, j)
                for k in range(2):
                    pe.transpose(bank[:, 0, k * P:(k + 1) * P], ext[:, k, STATE + P:STATE + PROMPT], ident[:])
                    last = pe.transpose(bank[:, 0, 256 + k * P:256 + (k + 1) * P], u_dense[:, k], ident[:])
                last.then_inc(uT_done, 1)
                if j < 7:
                    turn_history(j + 1)
                if j >= 2 and j % 2 == 0:
                    map_group(j // 2 - 1)
            map_group(3)
            pe.wait_ge(residual_taken, R_FFN1)
            norm_stats(3)
            with pe.Fori(0, CHUNKS) as c:
                ffn_chunk(W_FFN1 + c * 3, c + CHUNKS, R_FFN1 + c * 4, 8, False)

            for i in range(12):
                t, q = i % TT, i // TT
                if i == 0:
                    pe.wait_ge(residual_taken, R_END)
                if i >= 6:
                    pe.wait_ge(y_act if i % 2 else y_dve, (i - 6) // 2 + 1)
                for k in range(4):
                    last = pe.transpose(bank[:, i % 6, k * P:(k + 1) * P], x[:, 4 * q + k, t * P:(t + 1) * P], ident[:])
                last.then_inc(yT_done, 1)


INPUTS = ["x_prompt", "x_sample", "c_prompt", "c_sample", "cache_k", "cache_v", "state_pool", "w_ada",
          "b_ada", "g_mix", "g_ffn", "w_qkv", "g_q", "g_k", "w_o", "w_pool", "pool_scale", "w_gate",
          "w_up", "w_down"]
OUTPUTS = [(1, PROMPT, D), (STREAMS, STEP, D), (1, 1, PROMPT, NH, HD), (1, 1, PROMPT, NH, HD),
           (1, 1, STATE, D), (1, STREAMS, STEP, NH, HD), (1, STREAMS, STEP, NH, HD),
           (1, STREAMS, STATE, D)]


def kernel(**inputs):
    import concourse.bacc as bacc
    from concourse.bass_utils import run_bass_kernel_spmd

    nc = bacc.Bacc("TRN2", target_bir_lowering=False, num_devices=1)
    arrays, args = {}, []
    for name in INPUTS:
        a = np.ascontiguousarray(inputs[name])
        arrays[f"in_{name}"] = a
        args.append(nc.dram_tensor(f"in_{name}", a.shape, mybir.dt.from_np(a.dtype), kind="ExternalInput").ap())
    for i, shape in enumerate(OUTPUTS):
        args.append(nc.dram_tensor(f"out_{i}", shape, f32, kind="ExternalOutput").ap())
    encoder_step(nc, *args)
    got = run_bass_kernel_spmd(nc, [arrays], core_ids=[0]).results[0]
    return tuple(got[f"out_{i}"] for i in range(len(OUTPUTS)))
```
